# Optimizing a Trainium2 kernel written in Bass

```python
import math
import jax, jax.numpy as jnp
from jax import lax
import numpy as np

D_MODEL = 2048
BATCH = 1
SEQ = 512
DEPTH = 1
DEC_BATCH = 8
DEC_SEQ = 8
PAST_LEN = 256
PAGE_SIZE = 128

D_ATT = D_MODEL // 2
HD_A = 64
H_A = D_ATT // (2 * HD_A)
H_M = 4
D_MV = D_MODEL // 2
DV_M = D_MV // H_M
DK_M = DV_M // 2
D_MQK = H_M * DK_M
CHUNK = 64
QBLK = 128
EPS = 1e-6
SPLITS = (D_ATT, D_ATT, D_ATT, D_ATT, D_MQK, D_MQK, D_MV, D_MV, D_MV, H_M, H_M, D_MODEL, D_MODEL)
D_IN = 4 * D_ATT + 2 * D_MQK + 3 * D_MV + 2 * H_M + 2 * D_MODEL

kernel_name = 'hybrid_diffattn_mlstm_step'

def rmsnorm(x, g):
    xf = x.astype(jnp.float32)
    xf = xf * lax.rsqrt(jnp.mean(xf * xf, axis=-1, keepdims=True) + EPS)
    return (xf * g.astype(jnp.float32)).astype(x.dtype)

def split_in(u):
    idx = [int(i) for i in np.cumsum(SPLITS)[:-1]]
    return jnp.split(u, idx, axis=-1)

def alibi_slopes():
    return 2.0 ** (-8.0 * jnp.arange(1, H_A + 1, dtype=jnp.float32) / H_A)

def diff_attention(q, k, v, q_pos, k_pos, lam):
    s = jnp.einsum('bqhcd,bkhcd->bhcqk', q.astype(jnp.float32), k.astype(jnp.float32)) * (HD_A ** -0.5)
    dist = (q_pos[:, None] - k_pos[None, :]).astype(jnp.float32)
    bias = -alibi_slopes()[:, None, None, None] * dist[None, None]
    s = jnp.where(k_pos[None, :] <= q_pos[:, None], s + bias, -jnp.inf)
    p = jax.nn.softmax(s, axis=-1)
    a = p[:, :, 0] - lam * p[:, :, 1]
    return jnp.einsum('bhqk,bkhe->bqhe', a.astype(v.dtype), v)

def mlstm_chunk(carry, xs):
    C, n, m = carry
    q, k, v, ig, lf = xs
    L = q.shape[2]
    b = jnp.cumsum(lf, axis=-1)
    a = b + m[..., None]
    causal = jnp.tril(jnp.ones((L, L), dtype=bool))
    dmat = jnp.where(causal, b[..., :, None] - b[..., None, :] + ig[..., None, :], -jnp.inf)
    m_t = jnp.maximum(a, jnp.max(dmat, axis=-1))
    s = jnp.einsum('bhtk,bhsk->bhts', q, k) * jnp.exp(dmat - m_t[..., None])
    inter = jnp.exp(a - m_t)
    num = inter[..., None] * jnp.einsum('bhtk,bhvk->bhtv', q, C) + jnp.einsum('bhts,bhsv->bhtv', s, v)
    den = inter * jnp.einsum('bhtk,bhk->bht', q, n) + jnp.sum(s, axis=-1)
    h = num / jnp.maximum(jnp.abs(den), jnp.exp(-m_t))[..., None]
    m_new = m_t[..., -1]
    wk = jnp.exp(b[..., -1:] - b + ig - m_new[..., None])
    decay = jnp.exp(a[..., -1] - m_new)
    C_new = decay[..., None, None] * C + jnp.einsum('bhs,bhsv,bhsk->bhvk', wk, v, k)
    n_new = decay[..., None] * n + jnp.einsum('bhs,bhsk->bhk', wk, k)
    return (C_new, n_new, m_new), h

def mlstm(q, k, v, ig, lf, C0, n0, m0):
    B, T = q.shape[:2]
    L = math.gcd(T, CHUNK)
    nc = T // L

    def to_chunks(x):
        x = jnp.moveaxis(x.astype(jnp.float32), 2, 1)
        x = x.reshape(x.shape[:2] + (nc, L) + x.shape[3:])
        return jnp.moveaxis(x, 2, 0)

    xs = (to_chunks(q), to_chunks(k), to_chunks(v), to_chunks(ig), to_chunks(lf))
    carry0 = (C0.astype(jnp.float32), n0.astype(jnp.float32), m0.astype(jnp.float32))
    (C1, n1, m1), h = lax.scan(mlstm_chunk, carry0, xs)
    h = jnp.moveaxis(h, 0, 2).reshape(B, H_M, T, DV_M)
    return jnp.transpose(h, (0, 2, 1, 3)).astype(q.dtype), C1, n1, m1

def attend_prompt(q, k_rows, v_rows, lam):
    B, T = q.shape[:2]
    nb = T // QBLK
    k = k_rows.reshape(B, T, H_A, 2, HD_A)
    pos = jnp.arange(T, dtype=jnp.int32)
    qb = jnp.moveaxis(q.reshape(B, nb, QBLK, H_A, 2, HD_A), 1, 0)
    pb = pos.reshape(nb, QBLK)
    out = lax.map(lambda args: diff_attention(args[0], k, v_rows, args[1], pos, lam), (qb, pb))
    return jnp.moveaxis(out, 0, 1).reshape(B, T, H_A, 2 * HD_A)

def attend_sample(q, k_rows, v_rows, lam, cache_k, cache_v, page_table):
    Bd, T = q.shape[:2]
    past_len = page_table.shape[1] * PAGE_SIZE
    k_past = cache_k[page_table].reshape(Bd, past_len, H_A, 2 * HD_A)
    v_past = cache_v[page_table].reshape(Bd, past_len, H_A, 2 * HD_A)
    k_all = jnp.concatenate([k_past.astype(k_rows.dtype), k_rows], axis=1).reshape(Bd, past_len + T, H_A, 2, HD_A)
    v_all = jnp.concatenate([v_past.astype(v_rows.dtype), v_rows], axis=1)
    q_pos = past_len + jnp.arange(T, dtype=jnp.int32)
    k_pos = jnp.arange(past_len + T, dtype=jnp.int32)
    return diff_attention(q, k_all, v_all, q_pos, k_pos, lam)

def sublayer(x, c, attend, C0, n0, m0, lam, lam_init, w_ada, b_ada, norm_pre, norm_post, w_in,
             b_igate, b_fgate, attn_head_norm, mlstm_head_norm, w_br_a, w_br_m, w_out):
    B, T, _ = x.shape
    mod = jax.nn.silu(c) @ w_ada + b_ada
    shift, scale, gate = jnp.split(mod[:, None, :], 3, axis=-1)
    h = rmsnorm(x, norm_pre) * (1 + scale) + shift
    u = h @ w_in
    q_a, k_a, v_a, z_a, q_m, k_m, v_m, o_m, z_m, i_m, f_m, g_a, g_m = split_in(u)
    q_a = q_a.reshape(B, T, H_A, 2, HD_A)
    k_rows = k_a.reshape(B, T, H_A, 2 * HD_A)
    v_rows = v_a.reshape(B, T, H_A, 2 * HD_A)
    att = attend(q_a, k_rows, v_rows, lam)
    att = rmsnorm(att, attn_head_norm.reshape(H_A, 2 * HD_A)) * (1 - lam_init)
    y_a = (att.reshape(B, T, D_ATT) * jax.nn.silu(z_a)) @ w_br_a
    qm = q_m.reshape(B, T, H_M, DK_M)
    km = k_m.reshape(B, T, H_M, DK_M) * (DK_M ** -0.5)
    vm = v_m.reshape(B, T, H_M, DV_M)
    ig = (i_m + b_igate).astype(jnp.float32)
    lf = jax.nn.log_sigmoid((f_m + b_fgate).astype(jnp.float32))
    hm, C1, n1, m1 = mlstm(qm, km, vm, ig, lf, C0, n0, m0)
    hm = rmsnorm(hm, mlstm_head_norm.reshape(H_M, DV_M)).reshape(B, T, D_MV)
    y_m = (jax.nn.sigmoid(o_m) * hm * jax.nn.silu(z_m)) @ w_br_m
    y = (jax.nn.sigmoid(g_a) * y_a + jax.nn.sigmoid(g_m) * y_m) @ w_out
    out = x + gate * rmsnorm(y, norm_post)
    return out, k_rows, v_rows, C1, n1, m1

def setup_inputs(seed: int = 0) -> dict:
    key = jax.random.key(seed)
    ks = jax.random.split(key, 28)
    n_pages = PAST_LEN // PAGE_SIZE
    n_used = DEC_BATCH * n_pages
    n_pool = n_used + max(1, n_used // 4)
    page_table = jax.random.permutation(ks[0], n_pool)[:n_used].astype(jnp.int32).reshape(DEC_BATCH, n_pages)
    nrm = jax.random.normal
    f32 = jnp.float32
    return {
        'x_prompt': nrm(ks[1], (BATCH, SEQ, D_MODEL), f32),
        'x_sample': nrm(ks[2], (DEC_BATCH, DEC_SEQ, D_MODEL), f32),
        'cache_k': nrm(ks[3], (DEPTH, n_pool, PAGE_SIZE, H_A, 2 * HD_A), f32),
        'cache_v': nrm(ks[4], (DEPTH, n_pool, PAGE_SIZE, H_A, 2 * HD_A), f32),
        'state_C': 0.1 * nrm(ks[5], (DEPTH, DEC_BATCH, H_M, DV_M, DK_M), f32),
        'state_n': 0.5 * nrm(ks[6], (DEPTH, DEC_BATCH, H_M, DK_M), f32),
        'state_m': nrm(ks[7], (DEPTH, DEC_BATCH, H_M), f32),
        'page_table': page_table,
        'c_prompt': nrm(ks[8], (BATCH, D_MODEL), f32),
        'c_sample': nrm(ks[9], (DEC_BATCH, D_MODEL), f32),
        'w_ada': 0.5 * D_MODEL ** -0.5 * nrm(ks[10], (DEPTH, D_MODEL, 3 * D_MODEL), f32),
        'b_ada': 0.02 * nrm(ks[11], (DEPTH, 3 * D_MODEL), f32),
        'norm_pre': 1.0 + 0.05 * nrm(ks[12], (DEPTH, D_MODEL), f32),
        'norm_post': 1.0 + 0.05 * nrm(ks[13], (DEPTH, D_MODEL), f32),
        'w_in': D_MODEL ** -0.5 * nrm(ks[14], (DEPTH, D_MODEL, D_IN), f32),
        'b_igate': 0.1 * nrm(ks[15], (DEPTH, H_M), f32),
        'b_fgate': jnp.linspace(3.0, 6.0, H_M, dtype=f32) + 0.1 * nrm(ks[16], (DEPTH, H_M), f32),
        'lambda_q1': 0.1 * nrm(ks[17], (DEPTH, HD_A), f32),
        'lambda_k1': 0.1 * nrm(ks[18], (DEPTH, HD_A), f32),
        'lambda_q2': 0.1 * nrm(ks[19], (DEPTH, HD_A), f32),
        'lambda_k2': 0.1 * nrm(ks[20], (DEPTH, HD_A), f32),
        'attn_head_norm': 1.0 + 0.05 * nrm(ks[21], (DEPTH, D_ATT), f32),
        'mlstm_head_norm': 1.0 + 0.05 * nrm(ks[22], (DEPTH, D_MV), f32),
        'w_br_a': D_ATT ** -0.5 * nrm(ks[23], (DEPTH, D_ATT, D_MODEL), f32),
        'w_br_m': D_MV ** -0.5 * nrm(ks[24], (DEPTH, D_MV, D_MODEL), f32),
        'w_out': D_MODEL ** -0.5 * nrm(ks[25], (DEPTH, D_MODEL, D_MODEL), f32),
    }

def reference(x_prompt, x_sample, cache_k, cache_v, state_C, state_n, state_m, page_table, c_prompt, c_sample,
              w_ada, b_ada, norm_pre, norm_post, w_in, b_igate, b_fgate, lambda_q1, lambda_k1, lambda_q2,
              lambda_k2, attn_head_norm, mlstm_head_norm, w_br_a, w_br_m, w_out):
    xp, xs = x_prompt, x_sample
    kp_l, vp_l, Cp_l, np_l, mp_l = [], [], [], [], []
    ks_l, vs_l, Cs_l, ns_l, ms_l = [], [], [], [], []
    for layer in range(DEPTH):
        lam_init = 0.8 - 0.6 * math.exp(-0.3 * layer)
        lam = (jnp.exp(jnp.dot(lambda_q1[layer], lambda_k1[layer]).astype(jnp.float32))
               - jnp.exp(jnp.dot(lambda_q2[layer], lambda_k2[layer]).astype(jnp.float32)) + lam_init)
        weights = (w_ada[layer], b_ada[layer], norm_pre[layer], norm_post[layer], w_in[layer], b_igate[layer],
                   b_fgate[layer], attn_head_norm[layer], mlstm_head_norm[layer], w_br_a[layer], w_br_m[layer],
                   w_out[layer])
        B = xp.shape[0]
        C0 = jnp.zeros((B, H_M, DV_M, DK_M), jnp.float32)
        n0 = jnp.zeros((B, H_M, DK_M), jnp.float32)
        m0 = jnp.zeros((B, H_M), jnp.float32)
        xp, kp, vp, Cp, n_p, mp = sublayer(xp, c_prompt, attend_prompt, C0, n0, m0, lam, lam_init, *weights)
        ck, cv = cache_k[layer], cache_v[layer]
        att_s = lambda q, k, v, lm: attend_sample(q, k, v, lm, ck, cv, page_table)
        xs, k_s, v_s, Cs, n_s, ms = sublayer(xs, c_sample, att_s, state_C[layer], state_n[layer], state_m[layer],
                                             lam, lam_init, *weights)
        kp_l.append(kp); vp_l.append(vp); Cp_l.append(Cp); np_l.append(n_p); mp_l.append(mp)
        ks_l.append(k_s); vs_l.append(v_s); Cs_l.append(Cs); ns_l.append(n_s); ms_l.append(ms)
    return (xp, xs,
            jnp.stack(kp_l), jnp.stack(vp_l), jnp.stack(Cp_l), jnp.stack(np_l), jnp.stack(mp_l),
            jnp.stack(ks_l), jnp.stack(vs_l), jnp.stack(Cs_l), jnp.stack(ns_l), jnp.stack(ms_l))


_drawn_inputs = setup_inputs


def setup_inputs(seed=0):
    import zlib

    import numpy as np

    out = dict(_drawn_inputs(seed))
    spreads = {}
    factors = {'norm_post': 3.851,
     'b_igate': 8.0,
     'lambda_q1': 4.645,
     'lambda_k1': 8.0,
     'lambda_q2': 8.0,
     'lambda_k2': 8.0,
     'attn_head_norm': 4.725,
     'mlstm_head_norm': 6.974}
    for name, (base, spread) in spreads.items():
        noise = np.random.default_rng([zlib.crc32(name.encode()), seed]).standard_normal(out[name].shape)
        drawn = base * np.exp(spread * noise) if base else spread * noise
        out[name] = __import__('jax').numpy.asarray(drawn.astype(out[name].dtype))
    for name, factor in factors.items():
        out[name] = (out[name] * factor).astype(out[name].dtype)
    return out
```

```python
import math
from contextlib import ExitStack

import concourse.bass as bass
from concourse import mybir

F32 = mybir.dt.float32
F32R = mybir.dt.float32r
I32 = mybir.dt.int32
ALU = mybir.AluOpType
ACT = mybir.ActivationFunctionType
AX = mybir.AxisListType

P = 128
D = 2048
KT = D // P
TP = 512
NB = 8
TS = 8
NS = NB * TS
T = TP + NS
HALF = T // 2
NT = TP // P
HA = 8
DH = 64
HM = 4
DV = 256
DATT = HA * P
DMV = HM * DV
DMQK = HM * P
PAGES = 2
EPS = 1e-6
LAM_INIT = 0.8 - 0.6 * math.exp(-0.3 * 0)
NEG = -1e30
SLOPE = [2.0 ** (-8.0 * (h + 1) / HA) for h in range(HA)]

COL_QA = 0
COL_KA = DATT
COL_VA = 2 * DATT
COL_ZA = 3 * DATT
COL_QM = 4 * DATT
COL_KM = COL_QM + DMQK
COL_VM = COL_KM + DMQK
COL_OM = COL_VM + DMV
COL_ZM = COL_OM + DMV
COL_IF = COL_ZM + DMV
COL_GA = COL_IF + 2 * HM
COL_GM = COL_GA + D

CW = 256
NG = KT // 2
LOOKAHEAD = 3
RING = 4
A0 = 11 * NG + 5
STEPS = HA * NT
ADA_A = 16
ADA_N = ADA_A * NG
PH_PAIRS = [(COL_QA, 4), (COL_KA, 4), (COL_VA, 4), (COL_QM, 4), (COL_VM, 4), (COL_ZA, 4), (COL_OM, 4), (COL_ZM, 4)]
PAIRS1 = 32
S_F = PAIRS1 * NG
FSPLIT = 24
S_G = S_F + 8 * FSPLIT
S_END = S_G + 8 * NG


class Tally:

    def __init__(self, sem):
        self.sem, self.base, self.k = sem, 0, 0

    def link(self, eng, ins):
        self.k += 1
        ins.then_inc(self.sem, 1)
        eng.wait_ge(self.sem, self.base + self.k)

    def enter(self, i, start, per):
        self.base += self.k
        self.k, self.kept = 0, self.base
        self.base = (i - start) * per + self.kept
        self.per = per

    def leave(self, count):
        assert self.k == self.per, (self.k, self.per)
        self.base, self.k = self.kept + count * self.per, 0


def build(nc, x_prompt, x_sample, cache_k, cache_v, state_C, state_n, state_m, page_table, c_prompt, c_sample,
          w_ada, b_ada, norm_pre, norm_post, w_in, b_igate, b_fgate, lambda_q1, lambda_k1, lambda_q2,
          lambda_k2, attn_head_norm, mlstm_head_norm, w_br_a, w_br_m, w_out,
          y_prompt, y_sample, k_prompt, v_prompt, C_prompt, n_prompt, m_prompt,
          k_sample, v_sample, C_sample, n_sample, m_sample):
    n_pool = cache_k.shape[1]
    w_ada2, w_in2 = w_ada[0], w_in[0]
    wba, wbm, wo = w_br_a[0], w_br_m[0], w_out[0]
    y_scratch = nc.dram_tensor("y_scratch", [KT, P, T], F32, kind="Internal").ap()

    ctx = ExitStack()
    with ctx:
        origin = (nc.sbuf_base + 63) // 64 * 64
        at = {}
        top = 0
        for name, words in (("h_hi", KT * T), ("h_lo", KT * T), ("w_raw", RING * 512), ("w_hi", RING * 512),
                            ("w_lo", RING * 512), ("R1", 8 * T), ("R2", 8 * T), ("R3", 5 * 1024), ("R4", 8 * T),
                            ("WORK", 5632), ("VS", 1216), ("ROWS", 1232), ("SMALL", 1280)):
            at[name] = top
            top += words
        assert origin + 4 * top <= nc.sbuf_usable_end, (origin + 4 * top, nc.sbuf_usable_end)

        def sb(name, region, off, shape, dt=F32):
            return nc.alloc_sbuf_tensor_at(name, shape, dt, offset=origin + 4 * (at[region] + off))

        def ps(name, shape):
            return ctx.enter_context(nc.psum_tensor(name, shape, F32))

        def sem(name):
            return ctx.enter_context(nc.semaphore(name))

        h_hi = sb("h_hi", "h_hi", 0, [P, KT, T], F32R)
        h_lo = sb("h_lo", "h_lo", 0, [P, KT, T], F32R)
        w_raw = sb("w_raw", "w_raw", 0, [P, RING, 2, CW])
        w_hi = sb("w_hi", "w_hi", 0, [P, RING, 2, CW], F32R)
        w_lo = sb("w_lo", "w_lo", 0, [P, RING, 2, CW], F32R)
        xn_t = sb("xn_t", "R1", 0, [P, KT, T])
        q_att = sb("q_att", "R1", 0, [P, HA, T])
        att = sb("att", "R1", 0, [P, HA, T])
        brm = sb("brm", "R1", 0, [P, 2, 8, T], F32R)
        brm_lo, brm_hi = brm[:, 0], brm[:, 1]
        k_att = sb("k_att", "R2", 0, [P, HA, T])
        k_page = sb("k_page", "R2", 0, [P, PAGES, DATT])
        v_page = sb("v_page", "R2", PAGES * DATT, [P, PAGES, DATT])
        hm = sb("hm", "R2", 0, [P, 8, T])
        x_tile = sb("x_tile", "R3", 0, [P, 2, D])
        v_att = sb("v_att", "R3", 0, [P, NT, DATT])
        v_mls = sb("v_mls", "R3", 0, [P, NT + 1, DMV])
        bra_hi = sb("bra_hi", "R3", 0, [P, 8, T], F32R)
        q_mls = sb("q_mls", "R4", 0, [P, HM, T])
        k_mls = sb("k_mls", "R4", HM * T, [P, HM, T])
        bra_lo = sb("bra_lo", "R4", 0, [P, 8, T], F32R)
        y_tok = sb("y_tok", "R1", 0, [P, NT + 1, D])
        x_again = sb("x_again", "R1", 5 * D, [P, 4, D])
        v_smp = sb("v_smp", "VS", 0, [NS, DATT])
        y_back = sb("y_back", "VS", 0, [P, 2, T])
        mod_ss = sb("mod_ss", "ROWS", 0, [P, 2 * KT, 9])
        row_negM = sb("row_negM", "ROWS", 0, [HM, TP])
        row_em = sb("row_em", "ROWS", TP, [HM, TP])
        row_s = sb("row_s", "ROWS", 2 * TP, [HM, 3 * NS + NB])

        small = [0]

        def sm(name, shape, dt=F32):
            n = 1
            for s in shape[1:]:
                n *= s
            t = sb(name, "SMALL", small[0], shape, dt)
            small[0] += (n + 7) // 8 * 8
            assert small[0] <= 1280
            return t

        ident = sm("ident", [P, P])
        ones = sm("ones", [P, P])
        mask = sm("mask", [P, P])
        mask_bd = sm("mask_bd", [NS, NS])
        seq_mask = sm("seq_mask", [NS, NB])
        vec_t = sm("vec_t", [P, 96])
        mod_g = sm("mod_g", [P, KT, 9])
        c_t = sm("c_t", [P, KT, 9])
        ssq = sm("ssq", [P, 8])
        rinv = sm("rinv", [P, 8])
        bias8 = sm("bias8", [P, 8])
        g_tok = sm("g_tok", [P, NT + 1, HM])
        wk_tok = sm("wk_tok", [P, NT + 1, HM])
        dec_tok = sm("dec_tok", [NB, HM])
        neglam = sm("neglam", [P, 8])
        g02 = sm("g02", [P, HA])
        m0 = sm("m0", [HM, NB])
        mx = sm("mx", [P, 2, 2])
        nmx = sm("nmx", [P, 2, 2])
        rsum = sm("rsum", [P, 2, 2])
        rrec = sm("rrec", [P, 2, 2])
        pages = sm("pages", [1, NB * PAGES], I32)
        m_out = sm("m_out", [HM, 1 + NB])
        s1 = sm("s1", [P, 2, 9])
        bias_new = sm("bias_new", [P, 120])
        qrow = sm("qrow", [P, 2])
        eps = sm("eps", [P, 1])
        neg_half = sm("neg_half", [P, 8])
        V_PRE, V_POST, V_ADA, V_HA, V_HM = 0, 16, 32, 80, 88

        work = [0]

        def wk(name, shape, dt=F32, off=None):
            n = 1
            for s in shape[1:]:
                n *= s
            if off is not None:
                work[0] = off
            t = sb(name, "WORK", work[0], shape, dt)
            work[0] += (n + 7) // 8 * 8
            assert work[0] <= 5632, (name, work[0])
            return t

        h_tmp = wk("h_tmp", [P, 2, T], off=0)
        sq_junk = wk("sq_junk", [P, D])
        c_rows = wk("c_rows", [9, D])
        w_if = wk("w_if", [P, KT, 8])
        vec_in = wk("vec_in", [96, P])
        c_th = sq_junk[0:9, :]
        mod_row = sb("mod_row", "WORK", 2 * T + D, [9, 2, CW])
        stage = wk("stage", [P, 2, T], off=0)
        k_tok = wk("k_tok", [P, NT + 1, P])
        tri = wk("tri", [P, TP])
        tri_bd = wk("tri_bd", [NS, NS])
        row_b = wk("row_b", [HM, T])
        row_g = wk("row_g", [HM, T])
        row_x = wk("row_x", [HM, T])
        row_y = wk("row_y", [HM, T])
        gt = wk("gt", [P, NT + 1, 8])
        lf = wk("lf", [P, NT + 1, HM])
        lf2 = wk("lf2", [P, NT + 1, HM])
        lam_v = wk("lam_v", [P, 4, DH])
        lam_p = wk("lam_p", [P, DH])
        lam_s = wk("lam_s", [P, 4])
        e_map = wk("e_map", [P, 2, 2, TP], off=2 * T)
        a_t = wk("a_t", [P, TP])
        alibi = wk("alibi", [P, TP])
        dist = wk("dist", [P, TP])
        k_smp = wk("k_smp", [P, HA, NS], off=5632 - HA * NS)
        k_t = wk("k_t", [P, 2, 4, PAGES * P], off=0)
        q_diag = wk("q_diag", [P, 8 * 144])
        bias_past = wk("bias_past", [P, PAGES * P])
        sq_att = wk("sq_att", [P, TP])
        v_stage = wk("v_stage", [P, 2, T])
        assert work[0] <= 5632 - HA * NS
        e_smp = sb("e_smp", "R2", 4096, [P, PAGES * P + NS])
        comb = sb("comb", "R2", 4416, [P, NS])
        comb_r = sb("comb_r", "R2", 4480, [P, NS])
        comb_m = sb("comb_m", "R2", 4544, [P, NS])
        a_smp = sb("a_smp", "VS", DATT, [P, 3, NS])
        z_act = wk("z_act", [P, 2, T], off=0)
        negM_b = wk("negM_b", [P, TP])
        em_b = wk("em_b", [P, TP])
        e_d = wk("e_d", [P, TP])
        s_t = wk("s_t", [P, 2, TP])
        hm_sq = wk("hm_sq", [P, 2, TP])
        kw_tok = wk("kw_tok", [P, NT, P], off=5632 - NT * P)
        c0 = [wk("c0_a", [P, 4, 2, P], off=2 * T), sb("c0_b", "ROWS", 0, [P, 4, 2, P])]
        kw_s = wk("kw_s", [NS, 4, P])
        n0 = wk("n0", [NB, HM, P])
        k_tok_s = wk("k_tok_s", [NS, P])
        row_bc = wk("row_bc", [P, 3 * NS + NB])
        s_ts = wk("s_ts", [NS, NS])
        e_ds = wk("e_ds", [NS, NS])
        assert work[0] <= 2 * T + 5 * TP
        c0_t = wk("c0_t", [P, 4, 2, P], off=2 * T + 5 * TP)
        o_smp = wk("o_smp", [P, 8, NS])
        assert work[0] <= 5632, work[0]
        qi = sb("qi", "VS", 0, [P, NS])
        qn = sb("qn", "VS", 64, [P, NS])
        d_s = sb("d_s", "VS", 128, [P, NS])
        n0_t = sb("n0_t", "VS", 192, [P, NB])
        wkm = sb("wkm", "VS", 200, [NS, NB])
        hs_sq = sb("hs_sq", "VS", 208, [P, 2, NS])
        n_row = sb("n_row", "VS", 336, [1, P])
        n_out = sb("n_out", "VS", 464, [NB, P])
        c_st = sb("c_st", "VS", 592, [P, 2, P])
        g_a = wk("g_a", [P, 2, T], off=0)
        g_m = wk("g_m", [P, 2, T])
        y_mix = wk("y_mix", [P, 2, T])
        y_add = wk("y_add", [P, 2, T])
        mod_row_g = wk("mod_row_g", [9, CW], off=5120)
        y_sq = wk("y_sq", [P, 2, T], off=0)
        y_gp = wk("y_gp", [P, 2, T])
        y_acc = wk("y_acc", [P, T])
        xs_again = wk("xs_again", [NS, D])

        gemm = ps("gemm", [P, 2, 2, 512])
        bank_s = ps("bank_s", [P, 2, 512])
        bank_a = ps("bank_a", [P, 512])
        bank_o = ps("bank_o", [P, 512])

        def block(cb):
            return gemm[:, cb, :, 0:HALF]

        def halves(ap):
            return ap.rearrange("p (a t) -> p a t", a=2)

        raw_ready = [sem(f"raw_ready{i}") for i in range(RING)]
        hi_ready = sem("hi_ready")
        lo_ready = sem("lo_ready")
        gemm_used = sem("gemm_used")
        block0_done = sem("block0_done")
        bank_free = [sem("bank0_free"), sem("bank1_free")]
        ada_used = sem("ada_used")
        row_out = sem("row_out")
        row_tp = sem("row_tp")
        mod_done = sem("mod_done")
        const_ready = sem("const_ready")
        pool_chain, dve_chain, act_chain = sem("pool_chain"), sem("dve_chain"), sem("act_chain")
        in_c, in_vec, in_small, in_wif, in_lam = sem("in_c"), sem("in_vec"), sem("in_small"), sem("in_wif"), sem("in_lam")
        in_x = [sem("in_x0"), sem("in_x1")]
        c_tanh, c_silu, c_done, ct_ready, vec_done = sem("c_tanh"), sem("c_silu"), sem("c_done"), sem("ct_ready"), sem("vec_done")
        x_sq, x_normed, x_tr, x_out_a, x_out_d = sem("x_sq"), sem("x_normed"), sem("x_tr"), sem("x_out_a"), sem("x_out_d")
        h_made, h_hi_made, h_lo_made, gates_mm = sem("h_made"), sem("h_hi_made"), sem("h_lo_made"), sem("gates_mm")
        k_kept = sem("k_kept")
        tok_ps = sem("tok_ps")
        tok_done = sem("tok_done")
        k_out = sem("k_out")
        kw_ready = sem("kw_ready")
        rows_max, x_ms, x_pow, fin_ms, fin_pow = sem("rows_max"), sem("x_ms"), sem("x_pow"), sem("fin_ms"), sem("fin_pow")
        an_r, mr_ready, sr_ready, sh_cp = sem("an_r"), sem("mr_ready"), sem("sr_ready"), sem("sh_cp")
        prod_ready, z_used = sem("prod_ready"), sem("z_used")
        dist_made, comb_base, comb_made, qd_zero = sem("dist_made"), sem("comb_base"), sem("comb_made"), sem("qd_zero")
        c_outs, v_out = [sem("c_out_a"), sem("c_out_b")], sem("v_out")
        lam_dot, lam_exp = sem("lam_dot"), sem("lam_exp")
        gate_abs, gate_exp, gate_ln1, gate_ln, lf_done = sem("gate_abs"), sem("gate_exp"), sem("gate_ln1"), sem("gate_ln"), sem("lf_done")
        rows_ps, rows_sb, rows_arg, rows_exp, rows_tok_ps, rows_tok = (
            sem("rows_ps"), sem("rows_sb"), sem("rows_arg"), sem("rows_exp"), sem("rows_tok_ps"), sem("rows_tok"))
        sc_ps, sc_max, sc_exp, a_ready, at_ps, at_sb, pv_ps, pv_sb = (
            sem("sc_ps"), sem("sc_max"), sem("sc_exp"), sem("a_ready"), sem("at_ps"), sem("at_sb"), sem("pv_ps"), sem("pv_sb"))
        ks_copied = sem("ks_copied")
        in_k, in_v = sem("in_k"), sem("in_v")
        kt_ps, kt_sb, qd_ready, ss_ps, ss_max, ss_exp, cr_ready, as_ps, as_sb, pvs_ps, pvs_sb = (
            sem("kt_ps"), sem("kt_sb"), sem("qd_ready"), sem("ss_ps"), sem("ss_max"), sem("ss_exp"),
            sem("cr_ready"), sem("as_ps"), sem("as_sb"), sem("pvs_ps"), sem("pvs_sb"))
        an_sq, an_ps, an_done, bias_made = sem("an_sq"), sem("an_ps"), sem("an_done"), sem("bias_made")
        bc_ps, bc_sb, mq_ps, me_pre, me_exp, ms_ready, mn_ps, mk_ps, mk_sb, mo_sq, mo_cp, mss_ps, mh_done, mst_ps, mst_sb, mst_out = (
            sem("bc_ps"), sem("bc_sb"), sem("mq_ps"), sem("me_pre"), sem("me_exp"), sem("ms_ready"), sem("mn_ps"),
            sem("mk_ps"), sem("mk_sb"), sem("mo_sq"), sem("mo_cp"), sem("mss_ps"), sem("mh_done"), sem("mst_ps"), sem("mst_sb"), sem("mst_out"))
        z_tanh, br_hi, br_lo = sem("z_tanh"), sem("br_hi"), sem("br_lo")
        in_n0, in_c0, sb_ps, sb_sb, se_pre, se_exp, sst_ready, ct_ps, ct_sb, cn_ps, c_new, c_out = (
            sem("in_n0"), [sem("in_c0a"), sem("in_c0b")], sem("sb_ps"), sem("sb_sb"), sem("se_pre"), sem("se_exp"), sem("sst_ready"),
            sem("ct_ps"), sem("ct_sb"), sem("cn_ps"), sem("c_new"), sem("c_out"))
        sn_ps, sn_sq, sss_ps, shm_done, n_new, n_outs = sem("sn_ps"), sem("sn_sq"), sem("sss_ps"), sem("shm_done"), sem("n_new"), sem("n_outs")
        g_tanh, mix_ready, y_stored, in_y, y_hi_made, y_lo_made = (
            sem("g_tanh"), sem("mix_ready"), sem("y_stored"), [sem("in_y0"), sem("in_y1")], sem("y_hi_made"), sem("y_lo_made"))
        gp_ready, yq_done, yg_done, yt_ps, yt_sb, acc_done, tot_ps, fin_done, in_xa, stores = (
            sem("gp_ready"), sem("yq_done"), sem("yg_done"), sem("yt_ps"), sem("yt_sb"), sem("acc_done"),
            sem("tot_ps"), sem("fin_done"), sem("in_xa"), sem("stores"))

        dve_t, act_t, pool_t = Tally(dve_chain), Tally(act_chain), Tally(pool_chain)
        in_state = sem("in_state")
        nc_block = ctx.enter_context(nc.Block())

        @nc_block.sync
        def _(sp):
            def load(src, row, col, slot, ):
                sp.dma_start(w_raw[:, slot], src[row:row + 2 * P, bass.ds(col, CW)]
                             .rearrange("(t p) c -> p t c", p=P)).then_inc(raw_ready[slot], 16)

            def ada_pair(p, first):
                col = p * CW if first else sp.snap(p * CW)
                for g in range(NG):
                    if not (first and g < RING):
                        sp.wait_ge(ada_used, p * NG + g - RING + 1)
                    load(w_ada2, g * 2 * P, col, g % RING)

            ada_pair(0, True)
            with sp.Fori(1, ADA_A) as p:
                ada_pair(p, False)

            def in_pair(p, col, first):
                for g in range(NG):
                    if first and g < RING:
                        sp.wait_ge(ada_used, ADA_N - RING + g + 1)
                    else:
                        sp.wait_ge(lo_ready, p * NG + g - RING + 1)
                    load(w_in2, g * 2 * P, col, g % RING)

            p = 0
            for n, (col, pairs) in enumerate(PH_PAIRS):
                start = p
                if n == 0:
                    in_pair(0, col, True)
                    start = 1
                with sp.Fori(start, p + pairs) as i:
                    in_pair(i, sp.snap(col + (i - p) * CW), False)
                p += pairs

            def branch_pair(i, n1):
                col_ada, col_ga, col_gm = (sp.snap(c + i * CW) for c in (2 * D, COL_GA, COL_GM))
                col_br = n1 * CW - CW
                for n in range(4 * NG):
                    k, r = n // 4, n % 4
                    if r == 3:
                        sp.wait_ge(ada_used, ADA_N + NG * i + k)
                        load(w_ada2, k * 2 * P, col_ada, 3)
                        continue
                    j = 3 * k + r
                    sp.wait_ge(lo_ready, S_F + FSPLIT * i + j - 2)
                    if j < 8:
                        load(w_in2, j * 2 * P, col_ga, r)
                    elif j < 16:
                        load(w_in2, (j - 8) * 2 * P, col_gm, r)
                    elif j < 20:
                        load(wba, (j - 16) * 2 * P, col_br, r)
                    else:
                        load(wbm, (j - 20) * 2 * P, col_br, r)

            with sp.Fori(1, 9) as i:
                branch_pair(i - 1, i)

            def out_pair(p, first):
                col = p * CW if first else sp.snap(p * CW)
                for g in range(NG):
                    if first and g < 3:
                        sp.wait_ge(lo_ready, S_G + g - 2)
                    elif first and g == 3:
                        sp.wait_ge(ada_used, ADA_N + 8 * NG)
                    else:
                        sp.wait_ge(lo_ready, S_G + p * NG + g - 3)
                    load(wo, g * 2 * P, col, g % RING)

            out_pair(0, True)
            with sp.Fori(1, 8) as p:
                out_pair(p, False)
            for tt in range(NT + 1):
                sp.wait_ge(fin_done, tt + 1)
                dst = y_prompt[0, tt * P:(tt + 1) * P, :] if tt < NT else y_sample.rearrange("b t d -> (b t) d")
                sp.dma_start(dst, y_tok[0:dst.shape[0], tt, :]).then_inc(stores, 16)
            sp.wait_ge(stores, 16 * (NT + 1))

        @nc_block.tensor
        def _(pe):
            def mm(out, lhsT, rhs, start=True, stop=True):
                return nc.tensor.matmul(out, lhsT, rhs, start=start, stop=stop, skip_group_check=True)

            def granule(slot, hi, lo, kt, first, last, free):
                done = None
                for cb in range(2):
                    if first and free is not None:
                        pe.wait_ge(bank_free[cb], free)
                    for t in range(2):
                        wh = w_hi[:, slot, t, cb * P:(cb + 1) * P]
                        wl = w_lo[:, slot, t, cb * P:(cb + 1) * P]
                        for n, (w, h) in enumerate(((wh, hi), (wh, lo), (wl, hi))):
                            for a in range(2):
                                done = mm(gemm[:, cb, a, 0:HALF], w, h[:, kt + t, a * HALF:(a + 1) * HALF],
                                          start=first and t == 0 and n == 0, stop=last and t == 1 and n == 2)
                    if last and cb == 0:
                        done.then_inc(block0_done, 1)
                done.then_inc(gemm_used, 1)

            def to_tokens(src, ready, free, dst=None):
                pe.wait_ge(*ready)
                pe.wait_ge(*free)
                for j in range(NT):
                    nc.tensor.transpose(bank_s[:, 0, j * P:(j + 1) * P], src[:, j * P:(j + 1) * P], ident[:])
                nc.tensor.transpose(bank_s[0:NS, 1, 0:P], src[:, TP:T], ident[:]).then_inc(dst, 1)

            def ada_granule(slot, g, n, bank, free):
                pe.wait_ge(raw_ready[slot], n)
                if g == 0 and free is not None:
                    pe.wait_ge(row_out, free)
                mm(bank, c_t[:, 2 * g, :], w_raw[:, slot, 0, :], start=g == 0, stop=False)
                mm(bank, c_t[:, 2 * g + 1, :], w_raw[:, slot, 1, :], start=False, stop=g == NG - 1).then_inc(ada_used, 1)

            def ada_rows(rows, n):
                pe.wait_ge(row_out, n + 1)
                if not isinstance(n, int) or n:
                    pe.wait_ge(mod_done, n)
                for cb in range(2):
                    done = mm(bank_o[:, 9 * cb:9 * cb + 9], rows[:, cb * P:(cb + 1) * P], ident[0:9, 0:9])
                done.then_inc(row_tp, 1)

            pe.wait_ge(const_ready, 2)
            pe.wait_ge(in_vec, 16 * 5)
            nc.tensor.transpose(bank_o[:, 0:96], vec_in[:], ident[0:96, 0:96]).then_inc(ct_ready, 1)
            pe.wait_ge(c_silu, 2)
            for kt in range(KT):
                done = nc.tensor.transpose(bank_a[:, kt * 9:(kt + 1) * 9], c_rows[:, kt * P:(kt + 1) * P], ident[0:9, 0:9])
            done.then_inc(ct_ready, 1)
            pe.wait_ge(c_done, 2)

            ada_banks = (bank_a[0:9, 0:CW], gemm[0:9, 1, 1, 0:CW])

            def ada_pair(p, odd):
                for g in range(NG):
                    ada_granule(g % RING, g, 16 * (2 * p + g // RING + 1), ada_banks[odd],
                                None if isinstance(p, int) and p < 2 else p - 1)
                    if g == 3 and not (isinstance(p, int) and p == 0):
                        ada_rows(mod_row[:, 1 - odd, :], p - 1)

            def x_to_features(tt):
                pe.wait_ge(x_normed, tt + 1)
                n = P if tt < NT else NS
                for q in range(4):
                    if tt or q > 1:
                        pe.wait_ge(x_out_a if q % 2 == 0 else x_out_d, 2 * tt + q // 2)
                    for j in range(4):
                        kt = 4 * q + j
                        done = nc.tensor.transpose(bank_s[:, q % 2, j * P:j * P + n],
                                                   x_tile[0:n, tt % 2, kt * P:(kt + 1) * P], ident[0:n, 0:n])
                    done.then_inc(x_tr, 1)

            for p in range(NT + 1):
                ada_pair(p, p % 2)
                x_to_features(p)
            with pe.Fori(0, 2) as n:
                for odd in (1, 0):
                    ada_pair(2 * n + NT + 2 - odd, odd)

            def gates(j, jk, start, stop):
                pe.wait_ge(h_made, j + 1)
                for t in range(2):
                    for tt in range(NT + 1):
                        n = P if tt < NT else NS
                        done = mm(bank_s[0:n, 1, tt * 8:(tt + 1) * 8], h_tmp[:, t, tt * P:tt * P + n],
                                  w_if[:, jk + t, :], start=start and t == 0 and tt == 0, stop=stop and t == 1)
                done.then_inc(gates_mm, 1)

            ada_pair(9, 1)
            pe.wait_ge(in_wif, 16)
            pe.wait_ge(x_out_d, 2 * (NT + 1))
            for p in range(10, ADA_A):
                ada_pair(p, p % 2)
                gates(p - 10, 2 * (p - 10), p == 10, False)
            ada_rows(mod_row[:, 1, :], ADA_A - 1)
            gates(6, 12, False, False)
            gates(7, 14, False, True)

            def in_granule(p, g, free):
                pe.wait_ge(lo_ready, NG * p + g + 1)
                granule(g % RING, h_hi, h_lo, 2 * g, g == 0, g == NG - 1, free)

            def k_or_v_pair(p, n, free):
                for g in range(NG):
                    in_granule(p, g, free)
                    if n is not None and g < 2:
                        to_tokens(stage[:, g, :], (bank_free[g], free), (tok_done, n + 1) if g else (k_kept, n + 2), tok_ps)

            pe.wait_ge(h_lo_made, KT)
            for g in range(NG):
                in_granule(0, g, None)
            with pe.Fori(1, 4) as p:
                for g in range(NG):
                    in_granule(p, g, p)
            k_or_v_pair(4, None, 4)
            pe.wait_ge(gate_abs, 1)
            pe.wait_ge(x_out_a, 2 * (NT + 1))
            with pe.Fori(5, 8) as p:
                k_or_v_pair(p, 2 * (p - 5), p)
            for g in range(NG):
                in_granule(8, g, 8)
                if g < 2:
                    to_tokens(stage[:, g, :], (bank_free[g], 8), (tok_done, 6 + g), tok_ps)
                if g == 4:
                    pe.wait_ge(lf_done, 1)
                    pe.wait_ge(tok_done, 8)
                    pe.wait_ge(const_ready, 3)
                    for i in range(NT):
                        mm(bank_o[0:HM, i * P:TP], lf[:, i, :], tri[:, 0:TP - i * P], start=i == 0, stop=i == NT - 1)
                    mm(bank_a[0:HM, 0:NS], lf[0:NS, NT, :], tri_bd[:])
                    for i in range(NT):
                        nc.tensor.transpose(bank_s[0:HM, 1, i * P:(i + 1) * P], gt[:, i, 0:HM], ident[:])
                    nc.tensor.transpose(bank_a[0:HM, NS:2 * NS], gt[0:NS, NT, 0:HM], ident[0:NS, 0:NS]).then_inc(rows_ps, 1)
            with pe.Fori(9, 11) as p:
                for g in range(NG):
                    in_granule(p, g, p)
                    if g < 2:
                        if g == 0:
                            pe.wait_ge(rows_sb, 1)
                        to_tokens(stage[:, g, :], (bank_free[g], p), (tok_done, 2 * (p - 5) + g), tok_ps)

            def scores(s):
                h, qb = s // NT, s % NT
                n = (qb + 1) * P
                if s:
                    pe.wait_ge(sc_max, s)
                for c in range(2):
                    done = mm(bank_s[:, c, 0:n], q_att[c * DH:(c + 1) * DH, h, qb * P:n], k_att[c * DH:(c + 1) * DH, h, 0:n])
                done.then_inc(sc_ps, 1)

            def weights_t(s):
                qb = s % NT
                pe.wait_ge(a_ready, s + 1)
                if s:
                    pe.wait_ge(at_sb, s)
                for kb in range(qb + 1):
                    done = nc.tensor.transpose(bank_a[:, kb * P:(kb + 1) * P], e_map[:, s % 2, 0, kb * P:(kb + 1) * P], ident[:])
                done.then_inc(at_ps, 1)

            def values(s):
                h, qb = s // NT, s % NT
                pe.wait_ge(at_sb, s + 1)
                if s:
                    pe.wait_ge(pv_sb, s)
                for kb in range(qb + 1):
                    done = mm(bank_o[:, 0:P], v_att[:, kb, h * P:(h + 1) * P], a_t[:, kb * P:(kb + 1) * P],
                              start=kb == 0, stop=kb == qb)
                done.then_inc(pv_ps, 1)


            for x in range(11 * NG, 16 * NG):
                p, g = x // NG, x % NG
                in_granule(p, g, p)
                if 0 <= x - A0 - 2 < STEPS:
                    weights_t(x - A0 - 2)
                if 0 <= x - A0 - 3 < STEPS:
                    values(x - A0 - 3)
                if p in (11, 12) and g < 2:
                    if p == 12:
                        pe.wait_ge(sc_max, x - A0)
                    to_tokens(stage[:, g, :], (bank_free[g], p), (tok_done, 2 * (p - 5) + g), tok_ps)
                    if p == 12:
                        pe.wait_ge(tok_done, 2 * (p - 5) + g + 1)
                if x == A0:
                    pe.wait_ge(k_kept, HA)
                if x == 11 * NG + 4:
                    pe.wait_ge(rows_exp, 1)
                    pe.wait_ge(tok_done, 14)
                    for i in range(NT + 1):
                        n = P if i < NT else NS
                        mm(bank_s[0:n, 1, 4 * i:4 * i + 4], row_g[:, i * P:i * P + n], ident[0:HM, 0:HM])
                        mm(bank_s[0:n, 1, 32 + 4 * i:36 + 4 * i], row_y[:, i * P:i * P + n], ident[0:HM, 0:HM])
                    mm(bank_s[0:NB, 1, 64:68], row_s[:, 3 * NS:3 * NS + NB], ident[0:HM, 0:HM]).then_inc(rows_tok_ps, 1)
                    pe.wait_ge(rows_tok, 1)
                if 0 <= x - A0 < STEPS:
                    scores(x - A0)

            def keys_t(b, half):
                pe.wait_ge(in_k, 32 * (b + 1))
                if b or half:
                    pe.wait_ge(kt_sb, 2 * b + half)
                if not half and b:
                    pe.wait_ge(an_done, b)
                if not b and not half:
                    pe.wait_ge(sc_max, STEPS)
                for j in range(4):
                    for pg in range(PAGES):
                        h = 4 * half + j
                        done = nc.tensor.transpose(bank_s[:, j // 2, (j % 2 * PAGES + pg) * P:(j % 2 * PAGES + pg + 1) * P],
                                                   k_page[:, pg, h * P:(h + 1) * P], ident[:])
                done.then_inc(kt_ps, 1)

            def scores_s(b):
                pe.wait_ge(qd_ready, 2 * b + 2)
                pe.wait_ge(kt_sb, 2 * b + 2)
                pe.wait_ge(dist_made, 1)
                if b:
                    pe.wait_ge(ss_max, b)
                else:
                    pe.wait_ge(at_sb, STEPS)
                for h in range(HA):
                    mm(bank_a[:, 0:PAGES * P], q_diag[:, h * P:(h + 1) * P], k_t[:, h // 4, h % 4, :], start=h == 0, stop=h == HA - 1)
                for h in range(HA):
                    done = mm(bank_a[:, PAGES * P:PAGES * P + NS], q_diag[:, h * P:(h + 1) * P], k_smp[:, h, :],
                              start=h == 0, stop=h == HA - 1)
                done.then_inc(ss_ps, 1)

            def weights_s(b):
                pe.wait_ge(ss_exp, b + 1)
                pe.wait_ge(cr_ready, b + 1)
                if b:
                    pe.wait_ge(pvs_sb, b)
                else:
                    pe.wait_ge(pv_sb, STEPS)
                for kb in range(PAGES):
                    mm(bank_o[:, kb * NS:(kb + 1) * NS], e_smp[:, kb * P:(kb + 1) * P], comb_r[:])
                mm(bank_o[0:NS, 2 * NS:3 * NS], e_smp[:, 2 * P:2 * P + NS], comb_r[:]).then_inc(as_ps, 1)

            def values_s(b):
                pe.wait_ge(as_sb, b + 1)
                pe.wait_ge(in_v, 32 * (b + 1))
                for h in range(HA):
                    out = bank_o[:, 256 + h * TS:256 + (h + 1) * TS]
                    for pg in range(PAGES):
                        mm(out, v_page[:, pg, h * P:(h + 1) * P], a_smp[:, pg, h * TS:(h + 1) * TS], start=pg == 0, stop=False)
                    done = mm(out, v_smp[:, h * P:(h + 1) * P], a_smp[0:NS, 2, h * TS:(h + 1) * TS], start=False)
                done.then_inc(pvs_ps, 1)

            def norm_sum(b, bank):
                pe.wait_ge(an_sq, b + 1)
                mm(bank, ones[:], sq_att[:]).then_inc(an_ps, 1)

            def mls_bcast(hd, rows, n):
                mm(bank_s[:, 0, 0:n], ident[0:HM, hd:hd + 1].to_broadcast([HM, P]), rows).then_inc(bc_ps, 1)

            def mls_keys(hd):
                for i in range(NT):
                    done = nc.tensor.transpose(bank_a[:, i * P:(i + 1) * P], k_mls[:, hd, i * P:(i + 1) * P], ident[:])
                done.then_inc(mk_ps, 1)

            def mls_qk(hd, i):
                if i:
                    pe.wait_ge(ms_ready, NT * hd + i)
                else:
                    pe.wait_ge(mk_sb, hd + 1)
                mm(bank_a[:, 0:TP - i * P], k_mls[:, hd, i * P:(i + 1) * P], q_mls[:, hd, i * P:TP]).then_inc(mq_ps, 1)

            def mls_num(hd, i):
                pe.wait_ge(ms_ready, NT * hd + i + 1)
                rhs = s_t[:, i % 2, 0:TP - i * P]
                for r in range(2):
                    mm(bank_s[:, r, i * P:TP], v_mls[:, i, hd * DV + r * P:hd * DV + (r + 1) * P], rhs, start=i == 0, stop=i == NT - 1)
                mm(bank_o[:, i * P:TP], ones[:], rhs, start=i == 0, stop=i == NT - 1).then_inc(mn_ps, 1)

            def mls_squares(hd):
                pe.wait_ge(mo_sq, hd + 1)
                mm(bank_a[:], ones[:], hm_sq[:, 0, :], stop=False)
                mm(bank_a[:], ones[:], hm_sq[:, 1, :], start=False).then_inc(mss_ps, 1)

            def mls_state(hd, bank):
                for r in range(2):
                    for i in range(NT):
                        mm(bank[:, r * P:(r + 1) * P], v_mls[:, i, hd * DV + r * P:hd * DV + (r + 1) * P], kw_tok[:, i, :],
                           start=i == 0, stop=i == NT - 1)
                for i in range(NT):
                    done = mm(bank[0:1, 2 * P:3 * P], ones[:, 0:1], kw_tok[:, i, :], start=i == 0, stop=i == NT - 1)
                done.then_inc(mst_ps, 1)

            for x in range(16 * NG, 24 * NG):
                p, g = x // NG, x % NG
                c, d = x - 16 * NG, x - 20 * NG
                in_granule(p, g, p)
                if 17 <= p <= 20 and g < 2:
                    n = 16 + 2 * (p - 17) + g
                    if c % 4 == 0:
                        pe.wait_ge(an_done, c // 4)
                    elif c < 32:
                        pe.wait_ge(kt_sb, 2 * (c // 4) + 1)
                    else:
                        pe.wait_ge(bc_sb, 1)
                    to_tokens(v_stage[:, g, :], (bank_free[g], p), (tok_done, n), tok_ps)
                    pe.wait_ge(tok_done, n + 1)
                if c % 4 == 0 and 1 <= c // 4 <= 8:
                    weights_s(c // 4 - 1)
                if c % 4 == 1 and 1 <= c // 4 <= 8:
                    values_s(c // 4 - 1)
                if c < 32:
                    b = c // 4
                    if c % 4 < 2:
                        keys_t(b, c % 4)
                    if c % 4 == 2:
                        scores_s(b)
                    if c % 4 == 3:
                        pe.wait_ge(kt_sb, 2 * b + 2)
                        norm_sum(b, bank_s[:, 0, :])
                if d == 2:
                    pe.wait_ge(pvs_sb, NB)
                    norm_sum(8, bank_o[:, :])
                if d >= 0:
                    hd, q = d // 8, d % 8
                    if q == 0:
                        if hd:
                            mls_squares(hd - 1)
                            pe.wait_ge(mo_cp, hd)
                        else:
                            pe.wait_ge(an_done, 8)
                        mls_bcast(hd, row_negM[:], TP)
                    if q == 1:
                        pe.wait_ge(bc_sb, 2 * hd + 1)
                        mls_bcast(hd, row_em[:], TP)
                        pe.wait_ge(ss_max, NB)
                        if hd:
                            mls_state(hd - 1, bank_o)
                            pe.wait_ge(mr_ready, hd)
                        mls_keys(hd)
                    if 2 <= q < 6:
                        if q == 3:
                            pe.wait_ge(bc_sb, 2 * hd + 2)
                            pe.wait_ge(an_done, 9)
                            if hd:
                                pe.wait_ge(mst_sb, hd)
                        if q > 2:
                            mls_num(hd, q - 3)
                        mls_qk(hd, q - 2)
                    if q == 6:
                        mls_num(hd, NT - 1)

            def smp_bcast(hd):
                mm(bank_s[:, 0, 0:3 * NS + NB], ident[0:HM, hd:hd + 1].to_broadcast([HM, P]), row_s[:])
                mm(bank_o[0:NS, 0:NS], k_mls[:, hd, TP:T], q_mls[:, hd, TP:T])
                nc.tensor.transpose(bank_o[0:NS, NS:NS + P], k_mls[:, hd, TP:T], ident[:])
                pe.wait_ge(in_n0, 16)
                nc.tensor.transpose(bank_o[:, 256:256 + NB], n0[:, hd, :], ident[0:NB, 0:NB]).then_inc(sb_ps, 1)

            def smp_states_t(hd, lot):
                pe.wait_ge(in_c0[lot], 64 * (hd + 1))
                for b in range(4):
                    for r in range(2):
                        done = nc.tensor.transpose(bank_s[:, b // 2, (b % 2 * 2 + r) * P:(b % 2 * 2 + r + 1) * P], c0[lot][:, b, r, :], ident[:])
                done.then_inc(ct_ps, 1)

            def smp_num(hd, lot):
                pe.wait_ge(sst_ready, hd + 1)
                pe.wait_ge(ct_sb, 2 * hd + lot + 1)
                for r in range(2):
                    for b in range(4):
                        q = (4 * lot + b) * TS
                        out = bank_a[:, r * NS + q:r * NS + q + TS]
                        mm(out, v_mls[0:NS, NT, hd * DV + r * P:hd * DV + (r + 1) * P], s_ts[:, q:q + TS], stop=False)
                        done = mm(out, c0_t[:, b, r, :], qi[:, q:q + TS], start=False)
                if lot:
                    out = bank_a[:, 2 * NS:3 * NS]
                    mm(out, ones[0:NS, :], s_ts[:], stop=False)
                    mm(out, ones[:], qn[:], start=False)
                    done = mm(bank_a[0:NB, 256:256 + P], wkm[:], k_tok_s[:])
                done.then_inc(sn_ps, 1)

            def smp_new(hd, lot):
                pe.wait_ge(kw_ready, 2 * hd + lot + 1)
                for r in range(2):
                    done = mm(bank_s[:, r, :], v_mls[0:NS, NT, hd * DV + r * P:hd * DV + (r + 1) * P],
                              kw_s[:].rearrange("p b k -> p (b k)"))
                done.then_inc(cn_ps, 1)

            for x in range(24 * NG, 28 * NG):
                p, g = x // NG, x % NG
                hd = p - 24
                in_granule(p, g, p)
                if g == 0:
                    if hd == 0:
                        mls_squares(HM - 1)
                        pe.wait_ge(mo_cp, HM)
                        mls_state(HM - 1, bank_s[:, 1, :])
                    else:
                        pe.wait_ge(c_new, 2 * hd)
                        pe.wait_ge(sr_ready, hd)
                    smp_bcast(hd)
                if g in (1, 4):
                    if g == 1:
                        pe.wait_ge(sb_sb, hd + 1)
                        pe.wait_ge(mst_sb, HM)
                    else:
                        pe.wait_ge(c_new, 2 * hd + 1)
                    smp_states_t(hd, g // 4)
                if g in (2, 5):
                    if g == 2:
                        if hd:
                            pe.wait_ge(shm_done, hd)
                            pe.wait_ge(n_new, hd)
                        else:
                            pe.wait_ge(mr_ready, HM)
                    smp_num(hd, g // 4)
                    smp_new(hd, g // 4)
                if g == 7:
                    pe.wait_ge(sn_sq, hd + 1)
                    mm(bank_o[:, 384:384 + NS], ones[:], hs_sq[:, 0, :], stop=False)
                    mm(bank_o[:, 384:384 + NS], ones[:], hs_sq[:, 1, :], start=False).then_inc(sss_ps, 1)

            with pe.Fori(28, 32) as p:
                for g in range(NG):
                    in_granule(p, g, p)

            def branch_pair(i):
                for j in range(FSPLIT):
                    pe.wait_ge(lo_ready, S_F + FSPLIT * i + j + 1)
                    free = 32 + 4 * i
                    if j < 16:
                        granule(j % RING, h_hi, h_lo, 2 * (j % 8), j % 8 == 0, j % 8 == 7, free + j // 8)
                    elif j < 20:
                        granule(j % RING, bra_hi, bra_lo, 2 * (j - 16), j == 16, j == 19, free + 2)
                    else:
                        granule(j % RING, brm_hi, brm_lo, 2 * (j - 20), j == 20, j == 23, free + 3)
                    if j % 3 == 0:
                        ada_granule(3, j // 3, 16 * (97 + 8 * i + j // 3), ada_banks[0], ADA_A + i)
                ada_rows(mod_row_g, ADA_A + i)

            pe.wait_ge(br_lo, 16)
            pe.wait_ge(shm_done, HM)
            with pe.Fori(0, 8) as i:
                branch_pair(i)

            def out_pair(p, first):
                for g in range(NG):
                    pe.wait_ge(lo_ready, S_G + NG * p + g + 1)
                    if first:
                        pe.wait_ge(y_lo_made, 2 * g + 2)
                    granule(g % RING, h_hi, h_lo, 2 * g, g == 0, g == NG - 1, 64 + p)
                    if g < 2 and not first:
                        to_tokens(y_gp[:, g, :], (bank_free[g], 64 + p), (yt_sb, 2 * p - 1) if g else (yq_done, 2 * p), yt_ps)

            out_pair(0, True)
            with pe.Fori(1, 8) as p:
                out_pair(p, False)
            for g in range(2):
                to_tokens(y_gp[:, g, :], (bank_free[g], 72), (yt_sb, 14 + g), yt_ps)
            pe.wait_ge(acc_done, KT)
            pe.wait_ge(mod_done, ADA_A + 8)
            for tt in range(NT + 1):
                n = P if tt < NT else NS
                done = mm(bank_a[0:n, tt:tt + 1], y_acc[:, tt * P:tt * P + n], ones[:, 0:1])
            done.then_inc(tot_ps, 1)

        @nc_block.scalar
        def _(act):
            def go(out, in_, func=ACT.Copy, **kw):
                return nc.scalar.activation(out, in_, func, **kw)

            def split_hi(slot, raw_slot, count, s):
                act.wait_ge(raw_ready[raw_slot], 16 * count)
                act.wait_ge(gemm_used, s - RING + 1)
                go(w_hi[:, slot], w_raw[:, raw_slot]).then_inc(hi_ready, 1)

            def ahead(p, g):
                n = g + LOOKAHEAD
                split_hi(n % RING, n % RING, 33 + 2 * p + n // RING, NG * p + n)

            def block_ready(p, cb):
                act.wait_ge(*((block0_done, p + 1) if cb == 0 else (gemm_used, NG * (p + 1))))

            def inv_root(dst, src, scale, signal):
                act_t.link(act, go(dst, src, ACT.Ln, scale=scale, bias=eps[:, 0:1]))
                go(dst, dst, ACT.Exp, scale=-0.5).then_inc(signal, 1)

            act.dma_start(c_rows[0:1, :], c_prompt).then_inc(in_c, 16)
            act.dma_start(c_rows[1:9, :], c_sample).then_inc(in_c, 16)
            for dst, src in ((V_PRE, norm_pre), (V_POST, norm_post), (V_ADA, b_ada), (V_HA, attn_head_norm), (V_HM, mlstm_head_norm)):
                n = src.shape[1] // P
                act.dma_start(vec_in[dst:dst + n, :], src[0].rearrange("(n p) -> n p", p=P)).then_inc(in_vec, 16)
            act.dma_start(w_if[:], w_in2[:, COL_IF:COL_IF + 8].rearrange("(k p) c -> p k c", p=P)).then_inc(in_wif, 16)
            act.dma_start(bias8[:, 0:HM], b_igate.to_broadcast([P, HM])).then_inc(in_small, 16)
            act.dma_start(bias8[:, HM:2 * HM], b_fgate.to_broadcast([P, HM])).then_inc(in_small, 16)
            act.dma_start(m0[:], state_m[0].rearrange("b h -> h b"), allow_slow_non_contiguous=True).then_inc(in_small, 16)
            act.dma_start(pages[:], page_table.rearrange("(a b) n -> a (b n)", a=1)).then_inc(in_small, 16)

            act.wait_ge(in_c, 32)
            go(c_th, c_rows[:], ACT.Tanh, scale=0.5).then_inc(c_tanh, 1)
            act.wait_ge(c_silu, 1)
            for tt in range(NT + 1):
                n = P if tt < NT else NS
                act.wait_ge(in_x[tt % 2], 16 * (tt // 2 + 1))
                if tt:
                    act.wait_ge(x_sq, tt)
                go(sq_junk[0:n, :], x_tile[0:n, tt % 2, :], ACT.Square, accum_out=ssq[0:n, tt:tt + 1]).then_inc(x_sq, 1)
                for q in (0, 2):
                    act.wait_ge(x_tr, 4 * tt + q + 1)
                    go(xn_t[:, 4 * q:4 * q + 4, tt * P:tt * P + n],
                       bank_s[:, 0, :].rearrange("p (k t) -> p k t", k=4)[:, :, 0:n]).then_inc(x_out_a, 1)
            for j in range(NG):
                act.wait_ge(h_made, j + 1)
                go(h_hi[:, 2 * j:2 * j + 2, :], h_tmp[:]).then_inc(h_hi_made, 1)
            for s in range(LOOKAHEAD):
                act.wait_ge(raw_ready[s], 16 * 33)
                go(w_hi[:, s], w_raw[:, s]).then_inc(hi_ready, 1)

            def to_stage(dst, p, cb, n, scale=1.0):
                block_ready(p, cb)
                act.wait_ge(tok_ps, n)
                go(halves(dst[:, cb, :]), block(cb), scale=scale).then_inc(bank_free[cb], 1)

            def q_pair(p):
                for g in range(NG):
                    if not (isinstance(p, int) and g == 0):
                        ahead(p, g)
                    else:
                        act.wait_ge(raw_ready[3], 16 * 33)
                        go(w_hi[:, 3], w_raw[:, 3]).then_inc(hi_ready, 1)
                for cb in range(2):
                    block_ready(p, cb)
                    go(halves(q_att[:, 2 * p + cb, :]), block(cb), scale=DH ** -0.5).then_inc(bank_free[cb], 1)

            q_pair(0)
            with act.Fori(1, 4) as p:
                q_pair(p)
            for g in range(NG):
                ahead(4, g)
                if g == 1:
                    act.wait_ge(gate_abs, 1)
                    go(lf[:], lf[:], ACT.Exp, scale=-1.0).then_inc(gate_exp, 1)
                    act.wait_ge(lam_dot, 1)
                    go(lam_s[:, 2:4], lam_s[:, 0:2], ACT.Exp).then_inc(lam_exp, 1)
                if g == 3:
                    act.wait_ge(gate_ln1, 1)
                    go(lf[:], lf[:], ACT.Ln).then_inc(gate_ln, 1)
            for cb in range(2):
                block_ready(4, cb)
                go(halves(stage[:, cb, :]), block(cb)).then_inc(bank_free[cb], 1)
            with act.Fori(5, 8) as p:
                for g in range(NG):
                    ahead(p, g)
                for cb in range(2):
                    act.wait_ge(k_kept, 2 * (p - 4) + cb - 1)
                    to_stage(stage, p, cb, 2 * (p - 4) + cb - 1)
            act.wait_ge(k_kept, HA)
            with act.Fori(8, 11) as p:
                for g in range(NG):
                    ahead(p, g)
                for cb in range(2):
                    to_stage(stage, p, cb, 2 * (p - 4) + cb - 1)


            for x in range(11 * NG, 16 * NG):
                p, g = x // NG, x % NG
                ahead(p, g)
                if x == 11 * NG:
                    act.wait_ge(rows_arg, 1)
                    go(row_em[:], row_x[:, 0:TP], ACT.Exp)
                    go(row_s[:, NS:2 * NS], row_x[:, TP:T], ACT.Exp)
                    go(row_s[:, 2 * NS:3 * NS + NB], row_s[:, 2 * NS:3 * NS + NB], ACT.Exp)
                    go(row_y[:], row_y[:], ACT.Exp).then_inc(rows_exp, 1)
                s = x - A0 - 3
                if 0 <= s < STEPS:
                    n = (s % NT + 1) * P
                    act.wait_ge(at_ps, s + 1)
                    if s:
                        act.wait_ge(pv_ps, s)
                    go(a_t[:, 0:n], bank_a[:, 0:n]).then_inc(at_sb, 1)
                s = x - A0 - 4
                if 0 <= s < STEPS:
                    act.wait_ge(pv_ps, s + 1)
                    go(att[:, s // NT, s % NT * P:(s % NT + 1) * P], bank_o[:, 0:P]).then_inc(pv_sb, 1)
                s = x - A0 - 1
                if 0 <= s < STEPS:
                    n = (s % NT + 1) * P
                    act.wait_ge(sc_max, s + 1)
                    for c in range(2):
                        done = go(e_map[:, s % 2, c, 0:n], e_map[:, s % 2, c, 0:n], ACT.Exp, bias=nmx[:, s % 2, c:c + 1],
                                  accum_out=rsum[:, s % 2, c:c + 1])
                    done.then_inc(sc_exp, 1)
                if g == NG - 1:
                    for cb in range(2):
                        block_ready(p, cb)
                        if p == 11:
                            act.wait_ge(tok_ps, 13 + cb)
                            dst, scale = stage[:, cb, :], 1.0
                        elif p < 14:
                            dst, scale = q_mls[:, 2 * (p - 12) + cb, :], 1.0
                        else:
                            dst, scale = k_mls[:, 2 * (p - 14) + cb, :], P ** -0.5
                        go(halves(dst), block(cb), scale=scale).then_inc(bank_free[cb], 1)

            for x in range(16 * NG, 24 * NG):
                p, g = x // NG, x % NG
                c, d = x - 16 * NG, x - 20 * NG
                ahead(p, g)
                if x == 16 * NG:
                    act.wait_ge(pv_ps, STEPS)
                    go(att[:, HA - 1, TP - P:TP], bank_o[:, 0:P]).then_inc(pv_sb, 1)
                b = c // 4
                if c < 32 and c % 4 in (1, 2):
                    half = c % 4 - 1
                    act.wait_ge(kt_ps, 2 * b + half + 1)
                    if b:
                        act.wait_ge(ss_ps, b)
                    else:
                        act.wait_ge(a_ready, STEPS)
                        act.wait_ge(at_ps, STEPS)
                    go(k_t[:, half].rearrange("p h t -> p (h t)").rearrange("p (a t) -> p a t", a=2), bank_s[:]).then_inc(kt_sb, 1)
                if c % 4 == 1 and 1 <= b <= NB:
                    act.wait_ge(as_ps, b)
                    go(a_smp[:, 0:2, :], bank_o[:, 0:2 * NS].rearrange("p (a t) -> p a t", a=2))
                    go(a_smp[0:NS, 2, :], bank_o[0:NS, 2 * NS:3 * NS]).then_inc(as_sb, 1)
                if c % 4 == 0 and 1 <= b <= NB:
                    act.wait_ge(an_ps, b)
                    inv_root(sq_att[:], bank_s[:, 0, :], 1.0 / P, an_r)
                if d == 3:
                    act.wait_ge(an_ps, 9)
                    inv_root(sq_att[:], bank_o[:], 1.0 / P, an_r)
                if c < 32 and c % 4 == 3:
                    act.wait_ge(ss_max, b + 1)
                    go(e_smp[:], e_smp[:], ACT.Exp, bias=nmx[:, 0, 0:1], accum_out=rsum[:, 0, 0:1]).then_inc(ss_exp, 1)
                    if b:
                        act.wait_ge(an_done, b)
                    else:
                        act.wait_ge(pv_sb, STEPS)
                    go(sq_att[:], att[:, b, 0:TP], ACT.Square).then_inc(an_sq, 1)
                if d == 2:
                    act.wait_ge(pvs_sb, NB)
                    act.wait_ge(an_done, 8)
                    go(sq_att[:].rearrange("p (h t) -> p h t", h=HA), att[:, :, TP:T], ACT.Square).then_inc(an_sq, 1)
                if d >= 0:
                    hd, q = d // 8, d % 8
                    if q == 1 and hd:
                        act.wait_ge(mss_ps, hd)
                        inv_root(hm_sq[:, 0, :], bank_a[:], 1.0 / DV, mr_ready)
                    if q == 2 and hd:
                        act.wait_ge(mst_ps, hd)
                        if hd > 1:
                            act.wait_ge(mst_out, 32 * (hd - 1))
                        go(c_st[:], bank_o[:, 0:2 * P].rearrange("p (r k) -> p r k", r=2))
                        go(n_row[:], bank_o[0:1, 2 * P:3 * P]).then_inc(mst_sb, 1)
                    if 2 <= q < 6:
                        i = q - 2
                        act.wait_ge(me_pre, NT * hd + i + 1)
                        done = go(e_d[:, 0:P], e_d[:, 0:P], ACT.Exp, bias=g_tok[:, i, hd:hd + 1])
                        if i < NT - 1:
                            done = go(e_d[:, P:TP - i * P], negM_b[:, (i + 1) * P:TP], ACT.Exp, bias=g_tok[:, i, hd:hd + 1])
                        done.then_inc(me_exp, 1)
                if g == NG - 1:
                    for cb in range(2):
                        block_ready(p, cb)
                        if p < 20:
                            act.wait_ge(tok_ps, 16 + 2 * (p - 16) + cb - 1)
                            if p == 16:
                                act.wait_ge(sc_max, STEPS)
                            go(halves(v_stage[:, cb, :]), block(cb)).then_inc(bank_free[cb], 1)
                        else:
                            if p > 20:
                                act.wait_ge(z_used, 2 * (p - 20) + cb - 1)
                            go(halves(z_act[:, cb, :]), block(cb), ACT.Tanh, scale=0.5).then_inc(z_tanh, 1)
                    if d >= 0:
                        act.wait_ge(mo_cp, d // 8 + 1)
                        act.wait_ge(mh_done, d // 8)
                        go(hm_sq[:], hm[:, 2 * (d // 8):2 * (d // 8) + 2, 0:TP], ACT.Square).then_inc(mo_sq, 1)

            for x in range(24 * NG, 28 * NG):
                p, g = x // NG, x % NG
                hd = p - 24
                ahead(p, g)
                if hd == 0 and g == 1:
                    act.wait_ge(mss_ps, HM)
                    inv_root(hm_sq[:, 0, :], bank_a[:], 1.0 / DV, mr_ready)
                    act.wait_ge(mst_ps, HM)
                    act.wait_ge(mst_out, 32 * (HM - 1))
                    go(c_st[:], bank_s[:, 1, 0:2 * P].rearrange("p (r k) -> p r k", r=2))
                    go(n_row[:], bank_s[0:1, 1, 2 * P:3 * P]).then_inc(mst_sb, 1)
                if hd and g == 0:
                    act.wait_ge(sss_ps, hd)
                    inv_root(d_s[:], bank_o[:, 384:384 + NS], 1.0 / DV, sr_ready)
                if g == 1:
                    act.wait_ge(se_pre, hd + 1)
                    go(e_ds[:], e_ds[:], ACT.Exp, bias=g_tok[0:NS, NT, hd:hd + 1]).then_inc(se_exp, 1)
                if g in (2, 5):
                    lot = g // 4
                    act.wait_ge(ct_ps, 2 * hd + lot + 1)
                    if hd or lot:
                        act.wait_ge(sn_ps, 2 * hd + lot)
                    else:
                        act.wait_ge(mh_done, HM)
                    go(c0_t[:].rearrange("p b r k -> p (b r k)").rearrange("p (a t) -> p a t", a=2), bank_s[:]).then_inc(ct_sb, 1)
                if g == 6:
                    act.wait_ge(sh_cp, hd + 1)
                    go(hs_sq[:], hm[:, 2 * hd:2 * hd + 2, TP:T], ACT.Square).then_inc(sn_sq, 1)
                if g == NG - 1:
                    for cb in range(2):
                        block_ready(p, cb)
                        act.wait_ge(z_used, 2 * (p - 20) + cb - 1)
                        go(halves(z_act[:, cb, :]), block(cb), ACT.Tanh, scale=0.5).then_inc(bank_free[cb], 1)

            act.wait_ge(sss_ps, HM)
            inv_root(d_s[:], bank_o[:, 384:384 + NS], 1.0 / DV, sr_ready)
            act.wait_ge(shm_done, HM)
            act.wait_ge(n_new, HM)
            act.wait_ge(c_new, 2 * HM)
            act.wait_ge(z_used, 16)
            with act.Fori(28, 32) as p:
                for g in range(NG):
                    ahead(p, g)
                    if g in (2, 4):
                        go(bra_hi[:, 2 * (p - 28) + g // 4, :], att[:, 2 * (p - 28) + g // 4, :]).then_inc(br_hi, 1)
                act.wait_ge(br_lo, 4 * (p - 28) + 2)
                for cb in range(2):
                    block_ready(p, cb)
                    go(halves(z_act[:, cb, :]), block(cb), ACT.Tanh, scale=0.5).then_inc(z_tanh, 1)
                for cb in range(2):
                    act.wait_ge(prod_ready, 2 * (p - 28) + cb + 1)
                    go(brm_hi[:, 2 * (p - 28) + cb, :], z_act[:, cb, :]).then_inc(br_hi, 1)

            def branch_pair(i, last):
                for j in range(FSPLIT):
                    n = j + LOOKAHEAD
                    split_hi(n % RING, n % 3, 97 + 8 * i + n // 3, S_F + FSPLIT * i + n)
                    if last and j >= 16 and j < 23:
                        for blk in range(2 * (j - 16), 2 * (j - 16) + 2):
                            y_hi(blk)
                    if j in (7, 15):
                        for cb in range(2):
                            act.wait_ge(*((block0_done, 33 + 4 * i + j // 8) if cb == 0 else (gemm_used, S_F + FSPLIT * i + j + 1)))
                            go(halves((g_a if j == 7 else g_m)[:, cb, :]), block(cb), ACT.Tanh, scale=0.5).then_inc(bank_free[cb], 1)

            def y_hi(blk):
                act.wait_ge(in_y[blk % 2], 16 * (blk // 2 + 1))
                if blk == 0:
                    act.wait_ge(gemm_used, S_F + FSPLIT * 7 + 16)
                go(h_hi[:, blk, :], y_back[:, blk % 2, :], scale=0.5).then_inc(y_hi_made, 1)

            act.wait_ge(c_outs[0], 64 * HM)
            with act.Fori(0, 7) as i:
                branch_pair(i, False)
            branch_pair(7, True)

            def out_pair(p, first, last):
                for g in range(NG):
                    n = g + LOOKAHEAD
                    if not (last and n >= NG):
                        split_hi(n % RING, n % RING, 161 + 2 * p + n // RING, S_G + NG * p + n)
                    if first and g == 2:
                        y_hi(14)
                        y_hi(15)
                    if not first and g in (1, 2):
                        tok_out(2 * (p - 1) + g - 1)
                for cb in range(2):
                    act.wait_ge(*((block0_done, 65 + p) if cb == 0 else (gemm_used, S_G + NG * (p + 1))))
                    if not first:
                        act.wait_ge(acc_done, 2 * p + cb - 1)
                    go(halves(y_sq[:, cb, :]), block(cb), ACT.Square).then_inc(yq_done, 1)

            def tok_out(blk):
                act.wait_ge(yt_ps, blk + 1)
                go(y_tok[:, 0:NT, bass.ds(blk * P, P)], bank_s[:, 0, :].rearrange("p (a k) -> p a k", a=NT))
                go(y_tok[0:NS, NT, bass.ds(blk * P, P)], bank_s[0:NS, 1, 0:P]).then_inc(yt_sb, 1)

            out_pair(0, True, False)
            with act.Fori(1, 7) as p:
                out_pair(p, False, False)
            out_pair(7, False, True)
            tok_out(14)
            tok_out(15)

        @nc_block.vector
        def _(dve):
            V = nc.vector

            def link(ins):
                dve_t.link(dve, ins)

            def split_lo(slot, raw_slot, s):
                dve.wait_ge(hi_ready, s + 1)
                V.tensor_tensor(w_lo[:, slot], w_raw[:, raw_slot], w_hi[:, slot], ALU.subtract).then_inc(lo_ready, 1)

            def ahead(p, g):
                n = g + LOOKAHEAD
                split_lo(n % RING, n % RING, NG * p + n)

            def bcast(ap, n):
                return ap.unsqueeze(2).to_broadcast([ap.shape[0], ap.shape[1], n])

            dve.wait_ge(c_tanh, 1)
            V.scalar_tensor_tensor(c_rows[:], c_th, 1.0, c_rows[:], ALU.add, ALU.mult).then_inc(c_silu, 1)
            dve.wait_ge(c_silu, 1)
            V.tensor_scalar(c_rows[:], c_rows[:], 0.5, None, ALU.mult).then_inc(c_silu, 1)
            dve.wait_ge(ct_ready, 1)
            V.tensor_copy(vec_t[:], bank_o[:, 0:96]).then_inc(c_done, 1)
            dve.wait_ge(ct_ready, 2)
            V.tensor_copy(c_t[:].rearrange("p k c -> p (k c)"), bank_a[:, 0:KT * 9]).then_inc(c_done, 1)
            dve.wait_ge(c_done, 2)

            def norm_x(tt):
                n = P if tt < NT else NS
                dve.wait_ge(x_sq, tt + 1)
                V.tensor_scalar(rinv[0:n, tt:tt + 1], ssq[0:n, tt:tt + 1], 1.0 / D, EPS, ALU.mult, ALU.add).then_inc(x_ms, 1)
                dve.wait_ge(x_pow, tt + 1)
                V.tensor_scalar(x_tile[0:n, tt % 2, :], x_tile[0:n, tt % 2, :], rinv[0:n, tt:tt + 1], None, ALU.mult)\
                 .then_inc(x_normed, 1)

            def row_copy(dst, bank, p):
                dve.wait_ge(ada_used, NG * (p + 1))
                V.tensor_copy(dst, bank).then_inc(row_out, 1)

            def mod_out(dst, blk, p, of):
                dve.wait_ge(row_tp, p + 1)
                for cb in range(2):
                    done = V.tensor_scalar(dst[:, blk + cb, :], bank_o[:, 9 * cb:9 * cb + 9], vec_t[:, bass.ds(of + blk + cb, 1)], None, ALU.add)
                done.then_inc(mod_done, 1)

            def ss_rows(p):
                row_copy(mod_row[:, p % 2, :], (bank_a[0:9, 0:CW], gemm[0:9, 1, 1, 0:CW])[p % 2], p)

            for p in range(NT + 1):
                norm_x(p)
                if p:
                    mod_out(mod_ss, 2 * (p - 1), p - 1, V_ADA)
                ss_rows(p)
                n = P if p < NT else NS
                for q in (1, 3):
                    dve.wait_ge(x_tr, 4 * p + q + 1)
                    V.tensor_copy(xn_t[:, 4 * q:4 * q + 4, p * P:p * P + n],
                                  bank_s[:, 1, :].rearrange("p (k t) -> p k t", k=4)[:, :, 0:n]).then_inc(x_out_d, 1)
            for p in range(NT + 1, 9):
                mod_out(mod_ss, 2 * (p - 1), p - 1, V_ADA)
                ss_rows(p)
            dve.wait_ge(x_out_a, 2 * (NT + 1))
            dve.wait_ge(x_out_d, 2 * (NT + 1))
            for p in range(8, ADA_A):
                mod_out(mod_ss, 2 * p, p, V_ADA)
                dve.wait_ge(mod_done, p + 1)
                if p + 1 < ADA_A:
                    ss_rows(p + 1)
                j = p - 8
                for t in range(2):
                    kt = 2 * j + t
                    link(V.tensor_scalar(s1[:, t, :], mod_ss[:, KT + kt, :], 1.0, vec_t[:, V_PRE + kt:V_PRE + kt + 1], ALU.add, ALU.mult))
                if j:
                    dve.wait_ge(gates_mm, j)
                    dve.wait_ge(h_hi_made, j)
                    dve.wait_ge(h_lo_made, 2 * j)
                for t in range(2):
                    kt = 2 * j + t
                    x3 = xn_t[:, kt, TP:T].rearrange("p (b t) -> p b t", b=NB)
                    h3 = h_tmp[:, t, TP:T].rearrange("p (b t) -> p b t", b=NB)
                    V.tensor_scalar(h_tmp[:, t, 0:TP], xn_t[:, kt, 0:TP], s1[:, t, 0:1], mod_ss[:, kt, 0:1], ALU.mult, ALU.add)
                    link(V.tensor_tensor(h3, x3, bcast(s1[:, t, 1:9], TS), ALU.mult))
                    done = V.tensor_tensor(h3, h3, bcast(mod_ss[:, kt, 1:9], TS), ALU.add)
                done.then_inc(h_made, 1)
                dve.wait_ge(h_hi_made, j + 1)
                for t in range(2):
                    V.tensor_tensor(h_lo[:, 2 * j + t, :], h_tmp[:, t, :], h_hi[:, 2 * j + t, :], ALU.subtract).then_inc(h_lo_made, 1)
            for s in range(LOOKAHEAD):
                split_lo(s, s, s)

            for g in range(NG):
                ahead(0, g)
            with dve.Fori(1, 4) as p:
                for g in range(NG):
                    ahead(p, g)

            def keep(p, cb, blk):
                dve.wait_ge(bank_free[cb], p + 1)
                V.tensor_copy(k_att[:, blk, :], stage[:, cb, :]).then_inc(k_kept, 1)

            def tok_k(n):
                dve.wait_ge(tok_ps, n + 1)
                if not isinstance(n, int) or n:
                    dve.wait_ge(k_out, 32 * n)
                V.tensor_copy(k_tok[:, 0:NT, :], bank_s[:, 0, :].rearrange("p (a k) -> p a k", a=NT))
                V.tensor_copy(k_tok[0:NS, NT, :], bank_s[0:NS, 1, 0:P]).then_inc(tok_done, 1)

            def tok_v(prompt, sample, n, blk):
                dve.wait_ge(tok_ps, n + 1)
                V.tensor_copy(prompt[:, :, bass.ds(blk * P, P)], bank_s[:, 0, :].rearrange("p (a k) -> p a k", a=NT))
                V.tensor_copy(sample[:, bass.ds(blk * P, P)], bank_s[0:NS, 1, 0:P]).then_inc(tok_done, 1)

            for g in range(NG):
                ahead(4, g)
                if g == 0:
                    dve.wait_ge(gates_mm, NG)
                    dve.wait_ge(in_small, 64)
                    link(V.memset(gt[:], 0.0))
                    V.tensor_tensor(gt[:, 0:NT, :], bank_s[:, 1, 0:8 * NT].rearrange("p (a c) -> p a c", c=8),
                                    bias8[:].unsqueeze(1).to_broadcast([P, NT, 8]), ALU.add)
                    link(V.tensor_tensor(gt[0:NS, NT, :], bank_s[0:NS, 1, 8 * NT:8 * NT + 8], bias8[0:NS, :], ALU.add))
                    V.scalar_tensor_tensor(lf[:], gt[:, :, HM:8], -1.0, gt[:, :, HM:8], ALU.mult, ALU.max).then_inc(gate_abs, 1)
                    V.tensor_scalar(lf2[:], gt[:, :, HM:8], 0.0, None, ALU.min)
                    dve.wait_ge(in_lam, 64)
                    for n in range(2):
                        link(V.tensor_tensor(lam_p[:], lam_v[:, 2 * n, :], lam_v[:, 2 * n + 1, :], ALU.mult))
                        link(V.tensor_reduce(lam_s[:, n:n + 1], lam_p[:], AX.X, ALU.add))
                    V.tensor_scalar(g02[:], vec_t[:, V_HA:V_HA + HA], 1.0 - LAM_INIT, None, ALU.mult).then_inc(lam_dot, 1)
                if g == 2:
                    dve.wait_ge(gate_exp, 1)
                    V.tensor_scalar(lf[:], lf[:], 1.0, None, ALU.add).then_inc(gate_ln1, 1)
                    dve.wait_ge(lam_exp, 1)
                    link(V.tensor_tensor(neglam[:, 0:1], lam_s[:, 3:4], lam_s[:, 2:3], ALU.subtract))
                    link(V.tensor_scalar(neglam[:, 0:1], neglam[:, 0:1], -LAM_INIT, None, ALU.add))
                if g == 4:
                    dve.wait_ge(gate_ln, 1)
                    V.tensor_tensor(lf[:], lf2[:], lf[:], ALU.subtract).then_inc(lf_done, 1)
            for cb in range(2):
                keep(4, cb, cb)

            def k_pair(p):
                for g in range(NG):
                    ahead(p, g)
                    if g in (1, 2):
                        tok_k(2 * (p - 5) + g - 1)
                for cb in range(2):
                    keep(p, cb, 2 * (p - 4) + cb)

            k_pair(5)
            with dve.Fori(6, 8) as p:
                k_pair(p)

            def running_max(k, src, dst):
                V.tensor_copy(dst[:, 0:k], src[:, 0:k])
                d3, s3 = (r[:, TP:T].rearrange("p (b t) -> p b t", b=NB) for r in (dst, src))
                if k < TS:
                    V.tensor_copy(d3[:, :, 0:k], s3[:, :, 0:k])
                    V.tensor_tensor(d3[:, :, k:TS], s3[:, :, k:TS], s3[:, :, 0:TS - k], ALU.max)
                else:
                    V.tensor_copy(dst[:, TP:T], src[:, TP:T])
                link(V.tensor_tensor(dst[:, k:TP], src[:, k:TP], src[:, 0:TP - k], ALU.max))

            for g in range(NG):
                ahead(8, g)
                if g in (1, 2):
                    tok_k(6 + g - 1)
                if g == 5:
                    dve.wait_ge(rows_ps, 1)
                    link(V.tensor_copy(row_b[:, 0:TP], bank_o[0:HM, :]))
                    link(V.tensor_copy(row_b[:, TP:T], bank_a[0:HM, 0:NS]))
                    link(V.tensor_tensor(row_g[:, 0:TP], bank_s[0:HM, 1, :], row_b[:, 0:TP], ALU.subtract))
                    V.tensor_tensor(row_g[:, TP:T], bank_a[0:HM, NS:2 * NS], row_b[:, TP:T], ALU.subtract).then_inc(rows_sb, 1)
                    dve.wait_ge(rows_sb, 1)
                    running_max(1, row_g, row_x)
                    running_max(2, row_x, row_y)
                if g == 6:
                    running_max(4, row_y, row_x)
                    running_max(8, row_x, row_y)
                    running_max(16, row_y, row_x)
                if g == 7:
                    running_max(32, row_x, row_y)
                    running_max(64, row_y, row_x)
                    running_max(128, row_x, row_y)
                    running_max(256, row_y, row_x)
                    x3 = row_x[:, TP:T].rearrange("p (b t) -> p b t", b=NB)
                    link(V.tensor_scalar(row_x[:, 0:TP], row_x[:, 0:TP], 0.0, None, ALU.max))
                    V.tensor_tensor(x3, x3, bcast(m0[:], TS), ALU.max).then_inc(rows_max, 1)
            with dve.Fori(9, 11) as p:
                for g in range(NG):
                    ahead(p, g)
                    if g in (1, 2):
                        tok_v(v_att, v_smp, 2 * (p - 5) + g - 1, 2 * (p - 9) + g - 1)

            def mls_finish(hd):
                dve.wait_ge(mr_ready, hd + 1)
                for r in range(2):
                    blk = 2 * hd + r
                    done = V.scalar_tensor_tensor(hm[:, blk, 0:TP], hm[:, blk, 0:TP], vec_t[:, V_HM + blk:V_HM + blk + 1], hm_sq[:, 0, :],
                                                  ALU.mult, ALU.mult)
                done.then_inc(mh_done, 1)

            def weigh_keys(hd, lot):
                V.tensor_tensor(kw_s[:], k_tok_s[:].unsqueeze(1).to_broadcast([NS, 4, P]),
                                bcast(wkm[:, 4 * lot:4 * lot + 4], P), ALU.mult).then_inc(kw_ready, 1)

            def smp_finish(hd):
                dve.wait_ge(sr_ready, hd + 1)
                for r in range(2):
                    blk = 2 * hd + r
                    done = V.scalar_tensor_tensor(hm[:, blk, TP:T], hm[:, blk, TP:T], vec_t[:, V_HM + blk:V_HM + blk + 1], d_s[:],
                                                  ALU.mult, ALU.mult)
                done.then_inc(shm_done, 1)


            for x in range(11 * NG, 16 * NG):
                p, g = x // NG, x % NG
                ahead(p, g)
                if p in (11, 12) and g in (1, 2):
                    tok_v(v_att, v_smp, 2 * (p - 5) + g - 1, 2 * (p - 9) + g - 1)
                if x == 11 * NG + 5:
                    dve.wait_ge(rows_tok_ps, 1)
                    V.tensor_copy(g_tok[:, 0:NT, :], bank_s[:, 1, 0:16].rearrange("p (a h) -> p a h", h=HM))
                    V.tensor_copy(g_tok[0:NS, NT, :], bank_s[0:NS, 1, 16:20])
                    V.tensor_copy(wk_tok[:, 0:NT, :], bank_s[:, 1, 32:48].rearrange("p (a h) -> p a h", h=HM))
                    V.tensor_copy(wk_tok[0:NS, NT, :], bank_s[0:NS, 1, 48:52])
                    V.tensor_copy(dec_tok[:], bank_s[0:NB, 1, 64:68]).then_inc(rows_tok, 1)
                s = x - A0 - 2
                if 0 <= s < STEPS:
                    n = (s % NT + 1) * P
                    dve.wait_ge(sc_exp, s + 1)
                    link(V.reciprocal(rrec[:, s % 2, :], rsum[:, s % 2, :]))
                    link(V.tensor_scalar(rrec[:, s % 2, 1:2], rrec[:, s % 2, 1:2], neglam[:, 0:1], None, ALU.mult))
                    link(V.tensor_scalar(e_map[:, s % 2, 1, 0:n], e_map[:, s % 2, 1, 0:n], rrec[:, s % 2, 1:2], None, ALU.mult))
                    V.scalar_tensor_tensor(e_map[:, s % 2, 0, 0:n], e_map[:, s % 2, 0, 0:n], rrec[:, s % 2, 0:1],
                                           e_map[:, s % 2, 1, 0:n], ALU.mult, ALU.add).then_inc(a_ready, 1)
                s = x - A0 - 1
                if 0 <= s < STEPS:
                    n = (s % NT + 1) * P
                    if s == 0:
                        dve.wait_ge(dist_made, 1)
                        dve.wait_ge(k_out, 32 * HA)
                    if s % NT == 0:
                        link(V.tensor_scalar(alibi[:], dist[:], -SLOPE[s // NT], None, ALU.mult))
                    dve.wait_ge(sc_ps, s + 1)
                    if s > 1:
                        dve.wait_ge(at_ps, s - 1)
                    for c in range(2):
                        link(V.tensor_tensor(e_map[:, s % 2, c, 0:n], bank_s[:, c, 0:n], alibi[:, TP - n:TP], ALU.add))
                    link(V.tensor_reduce(mx[:, s % 2, :], e_map[:, s % 2, :, 0:n], AX.X, ALU.max))
                    V.tensor_scalar(nmx[:, s % 2, :], mx[:, s % 2, :], -1.0, None, ALU.mult).then_inc(sc_max, 1)

            for x in range(16 * NG, 24 * NG):
                p, g = x // NG, x % NG
                c, d = x - 16 * NG, x - 20 * NG
                ahead(p, g)
                b = c // 4
                if c % 4 == 0 and 1 <= b <= NB:
                    dve.wait_ge(ss_exp, b)
                    dve.wait_ge(comb_made, 1)
                    link(V.reciprocal(rrec[:, 0, 0:1], rsum[:, 0, 0:1]))
                    if b > 1:
                        dve.wait_ge(as_ps, b - 1)
                    V.tensor_scalar(comb_r[:], comb[:], rrec[:, 0, 0:1], None, ALU.mult).then_inc(cr_ready, 1)
                    dve.wait_ge(an_r, b)
                    V.scalar_tensor_tensor(att[:, b - 1, 0:TP], att[:, b - 1, 0:TP], g02[:, b - 1:b], sq_att[:], ALU.mult, ALU.mult)\
                     .then_inc(an_done, 1)
                if 17 <= p <= 20 and g in (0, 1) and d != 1:
                    tok_v(v_mls[:, 0:NT, :], v_mls[0:NS, NT, :], 16 + 2 * (p - 17) + g, 2 * (p - 17) + g)
                if c == 0:
                    dve.wait_ge(comb_base, 1)
                    link(V.tensor_tensor(e_smp[:, 0:NS], comb[:], comb_m[:], ALU.add))
                    link(V.tensor_tensor(e_smp[:, 0:NS], e_smp[:, 0:NS], comb_r[:], ALU.mult))
                    V.tensor_reduce(qrow[:, 0:1], e_smp[:, 0:NS], AX.X, ALU.add)
                    V.scalar_tensor_tensor(comb[:], comb_m[:], neglam[:, 0:1], comb[:], ALU.mult, ALU.add).then_inc(comb_made, 1)
                if c < 32 and c % 4 == 1:
                    if b:
                        dve.wait_ge(ss_ps, b)
                    else:
                        dve.wait_ge(qd_zero, 1)
                    for m in range(2):
                        V.tensor_copy(q_diag[m * DH:(m + 1) * DH, :].rearrange("p (h x) -> p h x", h=HA)[:, :, m * TS:(m + 1) * TS],
                                      q_att[m * DH:(m + 1) * DH, :, TP + b * TS:TP + (b + 1) * TS]).then_inc(qd_ready, 1)
                if c < 32 and c % 4 == 3:
                    dve.wait_ge(ss_ps, b + 1)
                    if b:
                        dve.wait_ge(as_ps, b)
                    dve.wait_ge(bias_made, 1)
                    V.tensor_tensor(e_smp[:, 0:PAGES * P], bank_a[:, 0:PAGES * P], bias_past[:], ALU.add)
                    link(V.tensor_tensor(e_smp[:, PAGES * P:PAGES * P + NS], bank_a[:, PAGES * P:PAGES * P + NS],
                                         bias_new[:, 56 - TS * b:120 - TS * b], ALU.add))
                    link(V.tensor_reduce(mx[:, 0, 0:1], e_smp[:], AX.X, ALU.max))
                    V.tensor_scalar(nmx[:, 0, 0:1], mx[:, 0, 0:1], -1.0, None, ALU.mult).then_inc(ss_max, 1)
                if c % 4 == 2 and 1 <= b <= NB:
                    dve.wait_ge(pvs_ps, b)
                    V.tensor_copy(att[:, :, TP + (b - 1) * TS:TP + b * TS],
                                  bank_o[:, 256:256 + NS].rearrange("p (h q) -> p h q", h=HA)).then_inc(pvs_sb, 1)
                if d == 3:
                    dve.wait_ge(an_r, 9)
                    sq3 = sq_att[:].rearrange("p (h t) -> p h t", h=HA)
                    link(V.tensor_tensor(sq3, sq3, bcast(g02[:], NS), ALU.mult))
                    V.tensor_tensor(att[:, :, TP:T], att[:, :, TP:T], sq3, ALU.mult).then_inc(an_done, 1)
                if d >= 0:
                    hd, q = d // 8, d % 8
                    if q == 1:
                        dve.wait_ge(bc_ps, 2 * hd + 1)
                        V.tensor_copy(negM_b[:], bank_s[:, 0, :]).then_inc(bc_sb, 1)
                        if d == 1:
                            tok_v(v_mls[:, 0:NT, :], v_mls[0:NS, NT, :], 23, 7)
                        if hd:
                            mls_finish(hd - 1)
                    if q == 2:
                        dve.wait_ge(bc_ps, 2 * hd + 2)
                        V.tensor_copy(em_b[:], bank_s[:, 0, :]).then_inc(bc_sb, 1)
                        dve.wait_ge(mk_ps, hd + 1)
                        if hd:
                            dve.wait_ge(mst_ps, hd)
                        for i in range(NT):
                            done = V.tensor_scalar(kw_tok[:, i, :], bank_a[:, i * P:(i + 1) * P], wk_tok[:, i, hd:hd + 1], None, ALU.mult)
                        done.then_inc(mk_sb, 1)
                    if 3 <= q < 7:
                        i = q - 3
                        dve.wait_ge(me_exp, NT * hd + i + 1)
                        dve.wait_ge(mq_ps, NT * hd + i + 1)
                        if NT * hd + i > 1:
                            dve.wait_ge(mn_ps, NT * hd + i - 1)
                        n = TP - i * P
                        V.tensor_tensor(s_t[:, i % 2, 0:n], bank_a[:, 0:n], e_d[:, 0:n], ALU.mult).then_inc(ms_ready, 1)
                    if 2 <= q < 6:
                        i = q - 2
                        if i == 0:
                            dve.wait_ge(bc_sb, 2 * hd + 1)
                        else:
                            dve.wait_ge(ms_ready, NT * hd + i)
                        V.tensor_tensor(e_d[:, 0:P], negM_b[:, i * P:(i + 1) * P], mask[:], ALU.add).then_inc(me_pre, 1)
                    if q == 7:
                        dve.wait_ge(mn_ps, NT * (hd + 1))
                        link(V.scalar_tensor_tensor(em_b[:], bank_o[:], -1.0, em_b[:], ALU.mult, ALU.max))
                        link(V.tensor_tensor(em_b[:], bank_o[:], em_b[:], ALU.max))
                        link(V.reciprocal(em_b[:], em_b[:]))
                        for r in range(2):
                            done = V.tensor_tensor(hm[:, 2 * hd + r, 0:TP], bank_s[:, r, :], em_b[:], ALU.mult)
                        done.then_inc(mo_cp, 1)
                if g == NG - 1 and p >= 20:
                    for cb in range(2):
                        blk = 2 * (p - 20) + cb
                        dve.wait_ge(z_tanh, blk + 1)
                        V.scalar_tensor_tensor(halves(z_act[:, cb, :]), halves(z_act[:, cb, :]), 1.0, block(cb), ALU.add, ALU.mult)\
                         .then_inc(bank_free[cb], 1)
                        dve.wait_ge(bank_free[cb], p + 1)
                        V.scalar_tensor_tensor(att[:, blk, :], z_act[:, cb, :], 0.5, att[:, blk, :], ALU.mult, ALU.mult).then_inc(z_used, 1)

            for x in range(24 * NG, 28 * NG):
                p, g = x // NG, x % NG
                hd = p - 24
                ahead(p, g)
                if g == 0 and hd:
                    smp_finish(hd - 1)
                if g == 2 and hd == 0:
                    mls_finish(HM - 1)
                if g == 1:
                    dve.wait_ge(sb_ps, hd + 1)
                    V.tensor_copy(row_bc[:], bank_s[:, 0, 0:3 * NS + NB]).then_inc(sb_sb, 1)
                    dve.wait_ge(sb_sb, hd + 1)
                    V.tensor_tensor(e_ds[:], row_bc[0:NS, 0:NS], mask_bd[:], ALU.add).then_inc(se_pre, 1)
                    V.tensor_copy(k_tok_s[:], bank_o[0:NS, NS:NS + P])
                    V.tensor_copy(n0_t[:], bank_o[:, 256:256 + NB])
                    V.tensor_scalar(wkm[:], seq_mask[:], wk_tok[0:NS, NT, hd:hd + 1], None, ALU.mult)
                    link(V.tensor_tensor(qi[:], q_mls[:, hd, TP:T], row_bc[:, 2 * NS:3 * NS], ALU.mult))
                    V.tensor_tensor(qn[:].rearrange("p (b t) -> p b t", b=NB), qi[:].rearrange("p (b t) -> p b t", b=NB),
                                    bcast(n0_t[:], TS), ALU.mult)
                    weigh_keys(hd, 0)
                    dve.wait_ge(se_exp, hd + 1)
                    V.tensor_tensor(s_ts[:], bank_o[0:NS, 0:NS], e_ds[:], ALU.mult).then_inc(sst_ready, 1)
                if g in (3, 6):
                    lot = g // 4
                    dve.wait_ge(cn_ps, 2 * hd + lot + 1)
                    if lot == 0:
                        weigh_keys(hd, 1)
                    for b in range(4):
                        done = V.scalar_tensor_tensor(c0[lot][:, b], c0[lot][:, b], row_bc[:, 3 * NS + 4 * lot + b:3 * NS + 4 * lot + b + 1],
                                                      bank_s[:, :, b * P:(b + 1) * P], ALU.mult, ALU.add)
                    done.then_inc(c_new, 1)
                if g == 6:
                    dve.wait_ge(sn_ps, 2 * hd + 2)
                    dve.wait_ge(n_outs, 16 * hd)
                    V.scalar_tensor_tensor(n_out[:], n0[:, hd, :], dec_tok[:, hd:hd + 1], bank_a[0:NB, 256:256 + P], ALU.mult, ALU.add)\
                     .then_inc(n_new, 1)
                    link(V.scalar_tensor_tensor(d_s[:], bank_a[:, 2 * NS:3 * NS], -1.0, row_bc[:, NS:2 * NS], ALU.mult, ALU.max))
                    link(V.tensor_tensor(d_s[:], bank_a[:, 2 * NS:3 * NS], d_s[:], ALU.max))
                    link(V.reciprocal(d_s[:], d_s[:]))
                    V.tensor_tensor(hm[:, 2 * hd:2 * hd + 2, TP:T], bank_a[:, 0:2 * NS].rearrange("p (r t) -> p r t", r=2),
                                    d_s[:].unsqueeze(1).to_broadcast([P, 2, NS]), ALU.mult).then_inc(sh_cp, 1)
                if g == NG - 1:
                    for cb in range(2):
                        blk = 2 * (p - 24) + cb
                        dve.wait_ge(bank_free[cb], p + 1)
                        V.tensor_scalar(o_smp[:, blk, :], z_act[:, cb, TP:T], 1.0, None, ALU.add)
                        V.scalar_tensor_tensor(hm[:, blk, 0:TP], z_act[:, cb, 0:TP], 1.0, hm[:, blk, 0:TP], ALU.add, ALU.mult).then_inc(z_used, 1)

            smp_finish(HM - 1)
            dve.wait_ge(z_used, 16)
            dve.wait_ge(shm_done, HM)
            link(V.tensor_tensor(hm[:, :, TP:T], hm[:, :, TP:T], o_smp[:], ALU.mult))
            with dve.Fori(28, 32) as p:
                for g in range(NG):
                    ahead(p, g)
                    if g in (2, 4):
                        dve.wait_ge(br_hi, 4 * (p - 28) + g // 2)
                        V.tensor_tensor(bra_lo[:, 2 * (p - 28) + g // 4, :], att[:, 2 * (p - 28) + g // 4, :],
                                        bra_hi[:, 2 * (p - 28) + g // 4, :], ALU.subtract).then_inc(br_lo, 1)
                for cb in range(2):
                    blk = 2 * (p - 28) + cb
                    dve.wait_ge(z_tanh, 2 * (p - 24) + cb + 1)
                    V.scalar_tensor_tensor(halves(z_act[:, cb, :]), halves(z_act[:, cb, :]), 1.0, block(cb), ALU.add, ALU.mult)\
                     .then_inc(bank_free[cb], 1)
                    dve.wait_ge(bank_free[cb], p + 1)
                    dve.wait_ge(br_lo, 4 * (p - 28) + 2)
                    V.scalar_tensor_tensor(z_act[:, cb, :], z_act[:, cb, :], 0.25, hm[:, blk, :], ALU.mult, ALU.mult).then_inc(prod_ready, 1)
                for cb in range(2):
                    blk = 2 * (p - 28) + cb
                    dve.wait_ge(br_hi, 4 * (p - 28) + 3 + cb)
                    V.tensor_tensor(brm_lo[:, blk, :], z_act[:, cb, :], brm_hi[:, blk, :], ALU.subtract).then_inc(br_lo, 1)

            def branch_pair(i, last):
                for j in range(FSPLIT):
                    n = j + LOOKAHEAD
                    split_lo(n % RING, n % 3, S_F + FSPLIT * i + n)
                    if last and 16 <= j < 23:
                        for blk in range(2 * (j - 16), 2 * (j - 16) + 2):
                            y_lo(blk)
                    if j == 22:
                        row_copy(mod_row_g[:], bank_a[0:9, 0:CW], ADA_A + i)
                    if j in (19, 23):
                        for cb in range(2):
                            dve.wait_ge(*((block0_done, 35 + 4 * i + (j == 23)) if cb == 0 else (gemm_used, S_F + FSPLIT * i + j + 1)))
                            if j == 19:
                                if not isinstance(i, int) or i:
                                    dve.wait_ge(y_stored, 32 * i)
                                dve.wait_ge(bank_free[cb], 33 + 4 * i)
                                V.scalar_tensor_tensor(halves(y_mix[:, cb, :]), halves(g_a[:, cb, :]), 1.0, block(cb), ALU.add, ALU.mult)\
                                 .then_inc(bank_free[cb], 1)
                            else:
                                dve.wait_ge(bank_free[cb], 35 + 4 * i)
                                V.scalar_tensor_tensor(halves(y_add[:, cb, :]), halves(g_m[:, cb, :]), 1.0, block(cb), ALU.add, ALU.mult)\
                                 .then_inc(bank_free[cb], 1)
                                dve.wait_ge(bank_free[cb], 36 + 4 * i)
                                V.tensor_tensor(y_mix[:, cb, :], y_mix[:, cb, :], y_add[:, cb, :], ALU.add).then_inc(mix_ready, 1)
                mod_out(mod_g, 2 * i, ADA_A + i, V_ADA + 2 * KT)

            def y_lo(blk):
                dve.wait_ge(y_hi_made, blk + 1)
                V.scalar_tensor_tensor(h_lo[:, blk, :], y_back[:, blk % 2, :], 0.5, h_hi[:, blk, :], ALU.mult, ALU.subtract)\
                 .then_inc(y_lo_made, 1)

            branch_pair(0, False)
            with dve.Fori(1, 7) as i:
                branch_pair(i, False)
            branch_pair(7, True)

            def out_pair(p, first, last):
                for g in range(NG):
                    n = g + LOOKAHEAD
                    if not (last and n >= NG):
                        split_lo(n % RING, n % RING, S_G + NG * p + n)
                    if first and g == 2:
                        y_lo(14)
                        y_lo(15)
                        dve.wait_ge(mod_done, ADA_A + 8)
                        link(V.tensor_tensor(mod_g[:], mod_g[:], bcast(vec_t[:, V_POST:V_POST + KT], 9), ALU.mult))
                        link(V.memset(y_acc[:], 0.0))
                for cb in range(2):
                    blk = 2 * p + cb
                    dve.wait_ge(yq_done, blk + 1)
                    if not first:
                        dve.wait_ge(yt_ps, 2 * p + cb - 1)
                    V.tensor_scalar(halves(y_gp[:, cb, :]), block(cb), mod_g[:, blk, 0:1], None, ALU.mult).then_inc(gp_ready, 1)
                    dve.wait_ge(gp_ready, blk + 1)
                    V.tensor_tensor(y_gp[:, cb, TP:T].rearrange("p (b t) -> p b t", b=NB),
                                    gemm[:, cb, 1, HALF - NS:HALF].rearrange("p (b t) -> p b t", b=NB),
                                    bcast(mod_g[:, blk, 1:9], TS), ALU.mult).then_inc(bank_free[cb], 1)
                    if not first or cb:
                        dve.wait_ge(acc_done, blk)
                    V.tensor_tensor(y_acc[:], y_acc[:], y_sq[:, cb, :], ALU.add).then_inc(acc_done, 1)

            out_pair(0, True, False)
            with dve.Fori(1, 7) as p:
                out_pair(p, False, False)
            out_pair(7, False, True)

            dve.wait_ge(tot_ps, 1)
            link(V.memset(rinv[:], 1.0))
            for tt in range(NT + 1):
                n = P if tt < NT else NS
                V.tensor_scalar(rinv[0:n, tt:tt + 1], bank_a[0:n, tt:tt + 1], 1.0 / D, EPS, ALU.mult, ALU.add)
            V.memset(ssq[:, 0:1], 0.0).then_inc(fin_ms, 1)
            dve.wait_ge(fin_pow, 1)
            dve.wait_ge(yt_sb, KT)
            dve.wait_ge(in_xa, 16 * (NT + 1))
            for tt in range(NT + 1):
                n = P if tt < NT else NS
                xa = x_again[:, tt, :] if tt < NT else xs_again[:]
                V.scalar_tensor_tensor(y_tok[0:n, tt, :], y_tok[0:n, tt, :], rinv[0:n, tt:tt + 1], xa, ALU.mult, ALU.add).then_inc(fin_done, 1)

        @nc_block.gpsimd
        def _(pool):
            G = nc.gpsimd

            def link(ins):
                pool_t.link(pool, ins)

            link(G.memset(ident[:], 0.0))
            G.memset(ones[:], 1.0)
            link(G.affine_select(out=ident[:], in_=ident[:], compare_op=ALU.not_equal, fill=1.0, base=0,
                                 pattern=[[-1, P]], channel_multiplier=1))
            link(G.memset(mask[:], 0.0))
            G.affine_select(out=mask[:], in_=mask[:], compare_op=ALU.is_ge, fill=NEG, base=0,
                            pattern=[[1, P]], channel_multiplier=-1).then_inc(const_ready, 1)

            G.memset(eps[:], EPS).then_inc(const_ready, 1)
            link(G.memset(neg_half[:], -0.5))

            def x_in(tt):
                src = x_prompt[0, tt * P:(tt + 1) * P, :] if tt < NT else x_sample.rearrange("b t d -> (b t) d")
                pool.dma_start(x_tile[0:src.shape[0], tt % 2, :], src).then_inc(in_x[tt % 2], 16)

            x_in(0)
            x_in(1)
            for tt in range(NT + 1):
                n = P if tt < NT else NS
                pool.wait_ge(x_ms, tt + 1)
                G.tensor_tensor(rinv[0:n, tt:tt + 1], rinv[0:n, tt:tt + 1], neg_half[0:n, 0:1], ALU.pow).then_inc(x_pow, 1)
                if tt + 2 <= NT:
                    pool.wait_ge(x_tr, 4 * (tt + 1))
                    x_in(tt + 2)

            link(G.memset(seq_mask[:], 1.0))
            link(G.affine_select(out=seq_mask[:], in_=seq_mask[:], compare_op=ALU.is_ge, fill=0.0, base=0,
                                 pattern=[[-TS, NB]], channel_multiplier=1))
            link(G.affine_select(out=seq_mask[:], in_=seq_mask[:], compare_op=ALU.is_ge, fill=0.0, base=TS - 1,
                                 pattern=[[TS, NB]], channel_multiplier=-1))
            link(G.memset(mask_bd[:], 0.0))
            bd = mask_bd[:].rearrange("p (b t) -> p b t", b=NB)
            link(G.affine_select(out=bd, in_=bd, compare_op=ALU.is_ge, fill=NEG, base=0,
                                 pattern=[[-TS, NB], [0, TS]], channel_multiplier=1))
            link(G.affine_select(out=bd, in_=bd, compare_op=ALU.is_ge, fill=NEG, base=0,
                                 pattern=[[TS, NB], [1, TS]], channel_multiplier=-1))
            pool.wait_ge(c_done, 2)
            pool.wait_ge(x_sq, NT + 1)
            for n, src in enumerate((lambda_q1, lambda_k1, lambda_q2, lambda_k2)):
                pool.dma_start(lam_v[:, n, :], src.to_broadcast([P, DH])).then_inc(in_lam, 16)
            link(G.memset(tri[:], 1.0))
            link(G.affine_select(out=tri[:], in_=tri[:], compare_op=ALU.is_ge, fill=0.0, base=0,
                                 pattern=[[1, TP]], channel_multiplier=-1))
            link(G.memset(tri_bd[:], 1.0))
            bd = tri_bd[:].rearrange("p (b t) -> p b t", b=NB)
            link(G.affine_select(out=bd, in_=bd, compare_op=ALU.is_ge, fill=0.0, base=0,
                                 pattern=[[-TS, NB], [0, TS]], channel_multiplier=1))
            G.affine_select(out=bd, in_=bd, compare_op=ALU.is_ge, fill=0.0, base=0,
                            pattern=[[TS, NB], [1, TS]], channel_multiplier=-1).then_inc(const_ready, 1)

            with pool.Fori(0, HA) as n:
                pool.wait_ge(tok_done, n + 1)
                pool.dma_start(k_prompt[0, 0].rearrange("(a p) h e -> p a h e", p=P)[:, :, bass.ds(n, 1), :].rearrange("p a h e -> p a (h e)"),
                               k_tok[:, 0:NT, :]).then_inc(k_out, 16)
                pool.dma_start(k_sample[0].rearrange("b t h e -> (b t) h e")[:, bass.ds(n, 1), :].rearrange("p h e -> p (h e)"),
                               k_tok[0:NS, NT, :]).then_inc(k_out, 16)

            pool.wait_ge(rows_max, 1)
            g3, y3 = (r[:, TP:T].rearrange("p (b t) -> p b t", b=NB) for r in (row_g, row_y))
            m3 = m0[:].unsqueeze(2).to_broadcast([HM, NB, TS])
            G.tensor_tensor(row_y[:], row_b[:], row_x[:], ALU.add)
            G.tensor_scalar(row_negM[:], row_x[:, 0:TP], -1.0, None, ALU.mult)
            link(G.tensor_scalar(row_s[:, 0:NS], row_x[:, TP:T], -1.0, None, ALU.mult))
            n3 = row_s[:, 0:NS].rearrange("p (b t) -> p b t", b=NB)
            G.tensor_copy(m_out[:, 0:1], row_y[:, TP - 1:TP])
            G.tensor_copy(m_out[:, 1:1 + NB], y3[:, :, TS - 1])
            G.tensor_tensor(row_s[:, 2 * NS:3 * NS].rearrange("p (b t) -> p b t", b=NB), m3, n3, ALU.add)
            G.tensor_tensor(row_s[:, 3 * NS:3 * NS + NB], m0[:], n3[:, :, TS - 1], ALU.add)
            link(G.tensor_scalar(row_x[:], row_y[:], -1.0, None, ALU.mult))
            G.tensor_scalar(row_y[:, 0:TP], row_g[:, 0:TP], row_negM[:, TP - 1:TP], None, ALU.add)
            G.tensor_tensor(y3, g3, n3[:, :, TS - 1:TS].to_broadcast([HM, NB, TS]), ALU.add).then_inc(rows_arg, 1)
            pool.wait_ge(rows_arg, 1)
            pool.dma_start(m_prompt[0, 0].rearrange("(h a) -> h a", a=1), m_out[:, 0:1]).then_inc(v_out, 16)
            pool.dma_start(m_sample[0].rearrange("b h -> h b"), m_out[:, 1:1 + NB], allow_slow_non_contiguous=True).then_inc(v_out, 16)

            pool.wait_ge(rows_tok, 1)
            link(G.iota(dist[:], pattern=[[-1, TP]], base=TP - P, channel_multiplier=1, allow_small_or_imprecise_dtypes=True))
            link(G.affine_select(out=dist[:], in_=dist[:], compare_op=ALU.is_ge, fill=-NEG, base=TP - P,
                                 pattern=[[-1, TP]], channel_multiplier=1))
            pool.wait_ge(k_kept, HA)
            link(G.tensor_copy(k_smp[:], k_att[:, :, TP:T]))
            G.memset(qrow[:, 0:1], 0.0).then_inc(dist_made, 1)

            pool.wait_ge(tok_done, 16)
            pool.dma_start(v_prompt[0, 0].rearrange("(a p) h e -> p a (h e)", p=P), v_att[:]).then_inc(v_out, 16)
            pool.dma_start(v_sample[0].rearrange("b t h e -> (b t) (h e)"), v_smp[:]).then_inc(v_out, 16)

            def page(cache, dst, b, s):
                for pg in range(PAGES):
                    n = PAGES * b + pg
                    at_page = pool.value_load(pages[0:1, n:n + 1], min_val=0, max_val=n_pool - 1)
                    pool.dma_start(dst[:, pg, :], cache[0, bass.ds(at_page, 1)].rearrange("a p h e -> p (a h e)")).then_inc(s, 16)

            pool.wait_ge(in_small, 64)
            pool.wait_ge(sc_ps, STEPS)
            page(cache_k, k_page, 0, in_k)
            page(cache_v, v_page, 0, in_v)
            pool.wait_ge(at_ps, STEPS)
            G.memset(q_diag[:], 0.0).then_inc(qd_zero, 1)
            G.memset(comb[:], 0.0)
            link(G.memset(comb_m[:], 0.0))
            for m, t in enumerate((comb, comb_m)):
                v = t[:].rearrange("p (h q) -> p h q", h=HA)
                done = G.affine_select(out=v, in_=v, compare_op=ALU.not_equal, fill=1.0, base=-TS * m,
                                       pattern=[[-2 * TS, HA], [-1, TS]], channel_multiplier=1)
            G.iota(comb_r[:].rearrange("p (h q) -> p h q", h=HA), pattern=[[0, HA], [1, TS]], base=0, channel_multiplier=0,
                   allow_small_or_imprecise_dtypes=True)
            link(done)
            G.memset(qrow[:, 0:1], 0.0).then_inc(comb_base, 1)
            link(G.memset(qrow[:, 1:2], -SLOPE[0]))
            for h in range(1, HA):
                link(G.affine_select(out=qrow[:, 1:2], in_=qrow[:, 1:2], compare_op=ALU.is_ge, fill=-SLOPE[h], base=2 * TS * h - 1,
                                     pattern=[[0, 1]], channel_multiplier=-1))
            pool.wait_ge(comb_made, 1)
            pool.wait_ge(pv_ps, STEPS)
            G.iota(bias_past[:], pattern=[[-1, PAGES * P]], base=PAGES * P, channel_multiplier=0, allow_small_or_imprecise_dtypes=True)
            link(G.iota(bias_new[:], pattern=[[-1, 120]], base=56, channel_multiplier=0, allow_small_or_imprecise_dtypes=True))
            G.tensor_scalar(bias_past[:], bias_past[:], qrow[:, 0:1], qrow[:, 1:2], ALU.add, ALU.mult)
            link(G.tensor_scalar(bias_new[:], bias_new[:], qrow[:, 0:1], None, ALU.add))
            link(G.tensor_scalar(sq_att[:, 0:120], bias_new[:], 0.0, NEG, ALU.is_lt, ALU.mult))
            link(G.tensor_scalar(bias_new[:], bias_new[:], qrow[:, 1:2], None, ALU.mult))
            link(G.tensor_tensor(bias_new[:], bias_new[:], sq_att[:, 0:120], ALU.add))
            G.affine_select(out=bias_new[:], in_=bias_new[:], compare_op=ALU.is_ge, fill=NEG, base=-56,
                            pattern=[[1, 120]], channel_multiplier=0).then_inc(bias_made, 1)
            for b in range(1, NB):
                pool.wait_ge(kt_ps, 2 * b)
                page(cache_k, k_page, b, in_k)
                pool.wait_ge(pvs_ps, b)
                page(cache_v, v_page, b, in_v)

            def state_in(hd, lot):
                for b in range(4):
                    pool.dma_start(c0[lot][:, b], state_C[0, 4 * lot + b, hd].rearrange("(r p) k -> p r k", p=P)).then_inc(in_c0[lot], 16)

            def y_store(i):
                for cb in range(2):
                    pool.dma_start(y_scratch[bass.ds(2 * i + cb, 1)].rearrange("a p t -> p (a t)"), y_mix[:, cb, :]).then_inc(y_stored, 16)

            def y_load(blk):
                if blk > 1:
                    pool.wait_ge(y_lo_made, blk - 1)
                pool.dma_start(y_back[:, blk % 2, :], y_scratch[blk]).then_inc(in_y[blk % 2], 16)

            for hd in range(HM):
                if hd == HM - 1:
                    pool.wait_ge(bc_ps, 2 * HM)
                    pool.wait_ge(bc_sb, 2 * HM)
                    state_in(0, 1)
                    pool.wait_ge(mo_cp, HM)
                    state_in(0, 0)
                    pool.dma_start(n0[:], state_n[0]).then_inc(in_n0, 16)
                pool.wait_ge(mst_sb, hd + 1)
                pool.dma_start(C_prompt[0, 0, hd].rearrange("(r p) k -> p r k", p=P), c_st[:]).then_inc(mst_out, 16)
                pool.dma_start(n_prompt[0, 0, hd].rearrange("(a k) -> a k", a=1), n_row[:]).then_inc(mst_out, 16)

            for hd in range(HM):
                for lot in range(2):
                    pool.wait_ge(c_new, 2 * hd + lot + 1)
                    for b in range(4):
                        pool.dma_start(C_sample[0, 4 * lot + b, hd].rearrange("(r p) k -> p r k", p=P), c0[lot][:, b]).then_inc(c_outs[lot], 16)
                    if hd < HM - 1:
                        pool.wait_ge(c_outs[lot], 64 * (hd + 1))
                        state_in(hd + 1, lot)
                pool.wait_ge(n_new, hd + 1)
                pool.dma_start(n_sample[0, :, hd, :], n_out[:]).then_inc(n_outs, 16)

            with pool.Fori(0, 7) as i:
                pool.wait_ge(mix_ready, 2 * i + 2)
                y_store(i)
            pool.wait_ge(y_stored, 16 * 14)
            for blk in range(14):
                y_load(blk)
            pool.wait_ge(mix_ready, KT)
            y_store(7)
            pool.wait_ge(y_stored, 16 * KT)
            for blk in range(14, KT):
                y_load(blk)
            pool.wait_ge(gemm_used, S_G)
            for tt in range(NT):
                pool.dma_start(x_again[:, tt, :], x_prompt[0, tt * P:(tt + 1) * P, :]).then_inc(in_xa, 16)
            pool.dma_start(xs_again[:], x_sample.rearrange("b t d -> (b t) d")).then_inc(in_xa, 16)
            pool.wait_ge(fin_ms, 1)
            G.tensor_tensor(rinv[:, 0:NT + 1], rinv[:, 0:NT + 1], neg_half[:, 0:NT + 1], ALU.pow).then_inc(fin_pow, 1)
            pool.wait_ge(k_out, 32 * HA)
            pool.wait_ge(v_out, 64)
            pool.wait_ge(mst_out, 32 * HM)
            pool.wait_ge(c_outs[0], 64 * HM)
            pool.wait_ge(c_outs[1], 64 * HM)
            pool.wait_ge(n_outs, 16 * HM)


_IN = ["x_prompt", "x_sample", "cache_k", "cache_v", "state_C", "state_n", "state_m", "page_table", "c_prompt", "c_sample",
       "w_ada", "b_ada", "norm_pre", "norm_post", "w_in", "b_igate", "b_fgate", "lambda_q1", "lambda_k1", "lambda_q2",
       "lambda_k2", "attn_head_norm", "mlstm_head_norm", "w_br_a", "w_br_m", "w_out"]
_OUT = [(1, TP, D), (NB, TS, D), (1, 1, TP, HA, P), (1, 1, TP, HA, P), (1, 1, HM, DV, P), (1, 1, HM, P), (1, 1, HM),
        (1, NB, TS, HA, P), (1, NB, TS, HA, P), (1, NB, HM, DV, P), (1, NB, HM, P), (1, NB, HM)]


def kernel(**inputs):
    import numpy as np
    from concourse.bacc import Bacc
    from concourse.bass_utils import run_bass_kernel_spmd

    nc = Bacc("TRN2", target_bir_lowering=False, num_devices=1)
    arrays, args = {}, []
    for name in _IN:
        a = np.ascontiguousarray(inputs[name])
        arrays["in_" + name] = a
        args.append(nc.dram_tensor("in_" + name, a.shape, mybir.dt.from_np(a.dtype), kind="ExternalInput").ap())
    for n, shape in enumerate(_OUT):
        args.append(nc.dram_tensor(f"out_{n}", shape, F32, kind="ExternalOutput").ap())
    build(nc, *args)
    r = run_bass_kernel_spmd(nc, [arrays], core_ids=[0])
    return tuple(r.results[0][f"out_{n}"] for n in range(len(_OUT)))
```
